# Optimizing a Trainium2 kernel written in Bass

```python
import jax, jax.numpy as jnp
from jax import lax
import numpy as np

D_MODEL = 1024
BATCH = 1
SEQ = 256
DEPTH = 1

GRID_W = 64
CTX_LEN = 256
HEAD_DIM = 64
NA_HEADS = 8
NA_WIN_R = 8
NA_WIN_C = 16
GQA_HEADS = 8
GQA_KV_HEADS = 2
Q_BLOCK = 128
ROPE_THETA = 10000.0
N_EXPERTS = 32
TOP_K = 4
D_FF = D_MODEL
SWIGLU_LIMIT = 7.0
SWIGLU_ALPHA = 1.702
EXPERT_BLOCK = 128
NORM_EPS = 1e-6

NA_WIDTH = NA_HEADS * HEAD_DIM
GQA_WIDTH = GQA_HEADS * HEAD_DIM
GQA_KV_WIDTH = GQA_KV_HEADS * HEAD_DIM
IN_SPLITS = (NA_WIDTH, NA_WIDTH, GQA_KV_WIDTH, GQA_KV_WIDTH, NA_WIDTH, GQA_WIDTH, D_MODEL, D_MODEL)
KV_COLS = 2 * NA_WIDTH + 2 * GQA_KV_WIDTH
IN_COLS = sum(IN_SPLITS)


def rmsnorm(x, g):
    xf = x.astype(jnp.float32)
    y = xf * lax.rsqrt(jnp.mean(xf * xf, axis=-1, keepdims=True) + NORM_EPS)
    return (y * g.astype(jnp.float32)).astype(x.dtype)

def split_cols(p, sizes):
    return jnp.split(p, np.cumsum(sizes)[:-1].tolist(), axis=-1)

def to_heads(t, n):
    return t.reshape(t.shape[0], t.shape[1], n, HEAD_DIM)

def axial_rope(x, row, col):
    half = HEAD_DIM // 2
    nf = half // 2
    freqs = ROPE_THETA ** (-jnp.arange(nf, dtype=jnp.float32) / nf)

    def rot(xp, pos):
        ang = pos.astype(jnp.float32)[:, None] * freqs
        cos = jnp.cos(ang)[None, :, None, :]
        sin = jnp.sin(ang)[None, :, None, :]
        x1 = xp[..., :nf].astype(jnp.float32)
        x2 = xp[..., nf:].astype(jnp.float32)
        return jnp.concatenate([x1 * cos - x2 * sin, x2 * cos + x1 * sin], axis=-1)

    return jnp.concatenate([rot(x[..., :half], row), rot(x[..., half:], col)], axis=-1).astype(x.dtype)

def gqa_attend(q, k, v):
    s = jnp.einsum('btkgd,bskd->bkgts', q, k)
    p = jax.nn.softmax(s.astype(jnp.float32), axis=-1).astype(q.dtype)
    return jnp.einsum('bkgts,bskd->btkgd', p, v)

def blocked_gqa(q, k, v):
    B, S = q.shape[0], q.shape[1]
    nb = S // Q_BLOCK
    qb = q.reshape(B, nb, Q_BLOCK, *q.shape[2:]).swapaxes(0, 1)
    out = lax.map(lambda blk: gqa_attend(blk, k, v), qb)
    return out.swapaxes(0, 1).reshape(B, S, -1)

def neighbourhood_attention(q, k, v, k_ctx, v_ctx, rpb):
    B, S, H, Dh = q.shape
    rows = S // GRID_W
    kr = min(NA_WIN_R, rows)
    kc = min(NA_WIN_C, GRID_W)
    qg = q.reshape(B, rows, GRID_W, H, Dh)
    kg = k.reshape(B, rows, GRID_W, H, Dh)
    vg = v.reshape(B, rows, GRID_W, H, Dh)
    cols = np.arange(GRID_W)
    c0 = np.clip(cols - kc // 2, 0, GRID_W - kc)
    col_idx = (c0[:, None] + np.arange(kc)[None, :]).astype(np.int32)
    col_off = (col_idx - cols[:, None] + (NA_WIN_C - 1)).astype(np.int32)

    def row_block(r):
        r0 = jnp.clip(r - kr // 2, 0, rows - kr)
        q_r = lax.dynamic_index_in_dim(qg, r, axis=1, keepdims=False)
        k_nb = lax.dynamic_slice_in_dim(kg, r0, kr, axis=1)[:, :, col_idx]
        v_nb = lax.dynamic_slice_in_dim(vg, r0, kr, axis=1)[:, :, col_idx]
        row_off = r0 + jnp.arange(kr, dtype=jnp.int32) - r + (NA_WIN_R - 1)
        bias = rpb[:, row_off[:, None, None], col_off[None, :, :]].transpose(0, 2, 1, 3)
        s_loc = jnp.einsum('bwhd,brwchd->bhwrc', q_r, k_nb) + bias.astype(q.dtype)
        s_ctx = jnp.einsum('bwhd,bnhd->bhwn', q_r, k_ctx)
        s = jnp.concatenate([s_loc.reshape(B, H, GRID_W, kr * kc), s_ctx], axis=-1)
        p = jax.nn.softmax(s.astype(jnp.float32), axis=-1).astype(q.dtype)
        p_loc = p[..., :kr * kc].reshape(B, H, GRID_W, kr, kc)
        p_ctx = p[..., kr * kc:]
        return (jnp.einsum('bhwrc,brwchd->bwhd', p_loc, v_nb)
                + jnp.einsum('bhwn,bnhd->bwhd', p_ctx, v_ctx))

    out = lax.map(row_block, jnp.arange(rows, dtype=jnp.int32))
    return out.transpose(1, 0, 2, 3, 4).reshape(B, S, H * Dh)

def merge_branches(o_a, o_b, g_a, g_b, w_out_a, w_out_b, w_o):
    return (jax.nn.sigmoid(g_a) * (o_a @ w_out_a) + jax.nn.sigmoid(g_b) * (o_b @ w_out_b)) @ w_o

def hybrid_mixer(h, h_ctx, w_in, rpb, g_qn, g_kn, w_out_a, w_out_b, w_o, row, col, update_ctx):
    B, S, _ = h.shape
    C = h_ctx.shape[1]
    scale = HEAD_DIM ** -0.5
    G = GQA_HEADS // GQA_KV_HEADS
    k_a, v_a, k_b, v_b, q_a, q_b, g_a, g_b = split_cols(h @ w_in, IN_SPLITS)
    if update_ctx:
        parts = split_cols(h_ctx @ w_in, IN_SPLITS)
    else:
        parts = split_cols(h_ctx @ w_in[:, :KV_COLS], IN_SPLITS[:4])
    k_ca = to_heads(parts[0], NA_HEADS)
    v_ca = to_heads(parts[1], NA_HEADS)
    k_cb = rmsnorm(to_heads(parts[2], GQA_KV_HEADS), g_kn)
    v_cb = to_heads(parts[3], GQA_KV_HEADS)

    o_a = neighbourhood_attention(to_heads(q_a, NA_HEADS) * scale, to_heads(k_a, NA_HEADS),
                                  to_heads(v_a, NA_HEADS), k_ca, v_ca, rpb)
    qb = axial_rope(rmsnorm(to_heads(q_b, GQA_HEADS), g_qn), row, col) * scale
    kb = axial_rope(rmsnorm(to_heads(k_b, GQA_KV_HEADS), g_kn), row, col)
    k_all = jnp.concatenate([kb, k_cb], axis=1)
    v_all = jnp.concatenate([to_heads(v_b, GQA_KV_HEADS), v_cb], axis=1)
    o_b = blocked_gqa(qb.reshape(B, S, GQA_KV_HEADS, G, HEAD_DIM), k_all, v_all)
    y = merge_branches(o_a, o_b, g_a, g_b, w_out_a, w_out_b, w_o)

    y_ctx = None
    if update_ctx:
        q_ca, q_cb, g_ca, g_cb = parts[4:]
        o_ca = gqa_attend(to_heads(q_ca, NA_HEADS)[:, :, :, None, :] * scale, k_ca, v_ca).reshape(B, C, -1)
        qcb = rmsnorm(to_heads(q_cb, GQA_HEADS), g_qn) * scale
        o_cb = gqa_attend(qcb.reshape(B, C, GQA_KV_HEADS, G, HEAD_DIM), k_cb, v_cb).reshape(B, C, -1)
        y_ctx = merge_branches(o_ca, o_cb, g_ca, g_cb, w_out_a, w_out_b, w_o)
    return y, y_ctx

def moe_ffn(h, w_router, b_router, w_gu, b_gu, w_dn, b_dn):
    T, D = h.shape
    logits = (h @ w_router + b_router).astype(jnp.float32)
    top_logits, top_e = lax.top_k(logits, TOP_K)
    top_w = jax.nn.softmax(top_logits, axis=-1).astype(h.dtype)
    n_assign = T * TOP_K
    flat_e = top_e.reshape(-1)
    flat_tok = jnp.arange(n_assign, dtype=jnp.int32) // TOP_K
    order = jnp.argsort(flat_e)
    e_sorted = flat_e[order]
    counts = jnp.bincount(flat_e, length=N_EXPERTS)
    padded = (counts + EXPERT_BLOCK - 1) // EXPERT_BLOCK * EXPERT_BLOCK
    pad_end = jnp.cumsum(padded)
    pad_start = pad_end - padded
    start = jnp.cumsum(counts) - counts
    dest = pad_start[e_sorted] + jnp.arange(n_assign, dtype=jnp.int32) - start[e_sorted]
    n_blocks = -(-n_assign // EXPERT_BLOCK) + N_EXPERTS
    n_slots = n_blocks * EXPERT_BLOCK
    slot_tok = jnp.full((n_slots,), T, dtype=jnp.int32).at[dest].set(flat_tok[order])
    slot_w = jnp.zeros((n_slots,), h.dtype).at[dest].set(top_w.reshape(-1)[order])
    block_e = jnp.minimum(jnp.searchsorted(pad_end, jnp.arange(n_blocks, dtype=jnp.int32) * EXPERT_BLOCK,
                                           side='right'), N_EXPERTS - 1)
    h_pad = jnp.concatenate([h, jnp.zeros((1, D), h.dtype)], axis=0)
    xb = h_pad[slot_tok].reshape(n_blocks, EXPERT_BLOCK, D)

    def expert_block(args):
        xe, e = args
        gu = xe @ w_gu[e] + b_gu[e]
        x_glu = jnp.minimum(gu[:, :D_FF], SWIGLU_LIMIT)
        x_lin = jnp.clip(gu[:, D_FF:], -SWIGLU_LIMIT, SWIGLU_LIMIT)
        act = (x_lin + 1) * (x_glu * jax.nn.sigmoid(SWIGLU_ALPHA * x_glu))
        return act @ w_dn[e] + b_dn[e]

    yb = lax.map(expert_block, (xb, block_e))
    y = jnp.zeros((T + 1, D), h.dtype).at[slot_tok].add(yb.reshape(n_slots, D) * slot_w[:, None])
    return y[:T]

def first_inputs(seed: int = 0) -> dict:
    key = jax.random.key(seed)
    ks = jax.random.split(key, 23)
    f32 = jnp.float32
    L = DEPTH

    def nrm(k, shape, s):
        return jax.random.normal(k, shape, f32) * s

    def gain(k, shape):
        return 1.0 + 0.05 * jax.random.normal(k, shape, f32)

    return {
        'x': nrm(ks[0], (BATCH, SEQ, D_MODEL), 1.0),
        'c': nrm(ks[1], (BATCH, D_MODEL), 1.0),
        'ctx': nrm(ks[2], (BATCH, CTX_LEN, D_MODEL), 1.0),
        'c_ctx': nrm(ks[3], (D_MODEL,), 1.0),
        'w_mod': nrm(ks[4], (L, D_MODEL, 6 * D_MODEL), 0.5 * D_MODEL ** -0.5),
        'b_mod': nrm(ks[5], (L, 6 * D_MODEL), 0.02),
        'g_pre_mix': gain(ks[6], (L, D_MODEL)),
        'g_post_mix': gain(ks[7], (L, D_MODEL)),
        'g_pre_ffn': gain(ks[8], (L, D_MODEL)),
        'g_post_ffn': gain(ks[9], (L, D_MODEL)),
        'w_in': nrm(ks[10], (L, D_MODEL, IN_COLS), D_MODEL ** -0.5),
        'rpb': nrm(ks[11], (L, NA_HEADS, 2 * NA_WIN_R - 1, 2 * NA_WIN_C - 1), 0.1),
        'g_qnorm': gain(ks[12], (L, HEAD_DIM)),
        'g_knorm': gain(ks[13], (L, HEAD_DIM)),
        'w_out_a': nrm(ks[14], (L, NA_WIDTH, D_MODEL), NA_WIDTH ** -0.5),
        'w_out_b': nrm(ks[15], (L, GQA_WIDTH, D_MODEL), GQA_WIDTH ** -0.5),
        'w_o': nrm(ks[16], (L, D_MODEL, D_MODEL), D_MODEL ** -0.5),
        'w_router': nrm(ks[17], (L, D_MODEL, N_EXPERTS), D_MODEL ** -0.5),
        'b_router': nrm(ks[18], (L, N_EXPERTS), 0.01),
        'w_gu': nrm(ks[19], (L, N_EXPERTS, D_MODEL, 2 * D_FF), D_MODEL ** -0.5),
        'b_gu': nrm(ks[20], (L, N_EXPERTS, 2 * D_FF), 0.02),
        'w_dn': nrm(ks[21], (L, N_EXPERTS, D_FF, D_MODEL), D_FF ** -0.5),
        'b_dn': nrm(ks[22], (L, N_EXPERTS, D_MODEL), 0.02),
    }

def first_block(x, c, ctx, c_ctx, w_mod, b_mod, g_pre_mix, g_post_mix, g_pre_ffn, g_post_ffn,
              w_in, rpb, g_qnorm, g_knorm, w_out_a, w_out_b, w_o,
              w_router, b_router, w_gu, b_gu, w_dn, b_dn):
    B, S, D = x.shape
    C = ctx.shape[1]
    t = jnp.arange(S, dtype=jnp.int32)
    row = t // GRID_W
    col = t % GRID_W
    silu_c = jax.nn.silu(c)
    silu_cc = jax.nn.silu(c_ctx)
    for i in range(DEPTH):
        update_ctx = i < DEPTH - 1
        sh1, sc1, gt1, sh2, sc2, gt2 = jnp.split((silu_c @ w_mod[i] + b_mod[i])[:, None, :], 6, axis=-1)
        n_mod = 6 if update_ctx else 2
        mod_c = jnp.split(silu_cc @ w_mod[i][:, :n_mod * D] + b_mod[i][:n_mod * D], n_mod)

        h = rmsnorm(x, g_pre_mix[i]) * (1 + sc1) + sh1
        h_ctx = rmsnorm(ctx, g_pre_mix[i]) * (1 + mod_c[1]) + mod_c[0]
        y, y_ctx = hybrid_mixer(h, h_ctx, w_in[i], rpb[i], g_qnorm[i], g_knorm[i],
                                w_out_a[i], w_out_b[i], w_o[i], row, col, update_ctx)
        x = x + gt1 * rmsnorm(y, g_post_mix[i])

        h2 = rmsnorm(x, g_pre_ffn[i]) * (1 + sc2) + sh2
        tokens = h2.reshape(B * S, D)
        if update_ctx:
            ctx = ctx + mod_c[2] * rmsnorm(y_ctx, g_post_mix[i])
            h2_ctx = rmsnorm(ctx, g_pre_ffn[i]) * (1 + mod_c[4]) + mod_c[3]
            tokens = jnp.concatenate([tokens, h2_ctx.reshape(B * C, D)], axis=0)
        f = moe_ffn(tokens, w_router[i], b_router[i], w_gu[i], b_gu[i], w_dn[i], b_dn[i])
        x = x + gt2 * rmsnorm(f[:B * S].reshape(B, S, D), g_post_ffn[i])
        if update_ctx:
            ctx = ctx + mod_c[5] * rmsnorm(f[B * S:].reshape(B, C, D), g_post_ffn[i])
    return x


CHUNK = 64
GLA_HEADS = 4
GLA_DK = 64
GLA_DV = 128
GLA_LOWRANK = 16
GLA_TAU = 16.0
FOX_HEADS = 8
FOX_HD = 64
D_FF_2 = 2816
CONV_W = 3
EPS = 1e-6

GLA_WIDTH = GLA_HEADS * GLA_DV
FOX_WIDTH = FOX_HEADS * FOX_HD
IN_SPLITS_2 = (GLA_HEADS * GLA_DK, GLA_HEADS * GLA_DK, GLA_WIDTH, GLA_WIDTH, GLA_LOWRANK,
             FOX_WIDTH, FOX_WIDTH, FOX_WIDTH, FOX_HEADS, D_MODEL, D_MODEL)
IN_COLS_2 = sum(IN_SPLITS_2)
IN_OFFSETS = tuple(int(v) for v in np.cumsum(IN_SPLITS_2)[:-1])


def rmsnorm_2(x, g):
    xf = x.astype(jnp.float32)
    y = xf * lax.rsqrt(jnp.mean(xf * xf, axis=-1, keepdims=True) + EPS)
    return (y * g.astype(jnp.float32)).astype(x.dtype)

def gla_chunked(q, k, v, log_a):
    B, S, H, dk = q.shape
    dv = v.shape[-1]
    n = S // CHUNK
    def blocks(t):
        return t.astype(jnp.float32).reshape(B, n, CHUNK, H, t.shape[-1]).transpose(0, 3, 1, 2, 4)
    qc, kc, vc, la = blocks(q), blocks(k), blocks(v), blocks(log_a)
    b = jnp.cumsum(la, axis=3)
    q_e = qc * jnp.exp(b)
    k_e = kc * jnp.exp(-b)
    causal = jnp.tril(jnp.ones((CHUNK, CHUNK), dtype=bool))
    scores = jnp.where(causal, jnp.einsum('bhnld,bhnmd->bhnlm', q_e, k_e), 0.0)
    o_intra = jnp.einsum('bhnlm,bhnmv->bhnlv', scores, vc)
    b_last = b[:, :, :, -1:, :]
    chunk_kv = jnp.einsum('bhnld,bhnlv->bhndv', kc * jnp.exp(b_last - b), vc)
    decay = jnp.exp(b_last[:, :, :, 0, :])

    def step(state, inp):
        dec, kv = inp
        return dec[..., None] * state + kv, state

    _, prev = lax.scan(step, jnp.zeros((B, H, dk, dv), jnp.float32),
                       (jnp.moveaxis(decay, 2, 0), jnp.moveaxis(chunk_kv, 2, 0)))
    prev = jnp.moveaxis(prev, 0, 2)
    o = o_intra + jnp.einsum('bhnld,bhndv->bhnlv', q_e, prev)
    return o.transpose(0, 2, 3, 1, 4).reshape(B, S, H, dv).astype(v.dtype)

def fox_attention(q, k, v, log_f):
    B, S, H, d = q.shape
    scale = d ** -0.5
    qh, kh, vh = (t.transpose(0, 2, 1, 3) for t in (q, k, v))
    c = jnp.cumsum(log_f.astype(jnp.float32), axis=1).transpose(0, 2, 1)
    outs = []
    for i in range(S // Q_BLOCK):
        lo, hi = i * Q_BLOCK, (i + 1) * Q_BLOCK
        logits = jnp.einsum('bhqd,bhkd->bhqk', qh[:, :, lo:hi], kh[:, :, :hi]).astype(jnp.float32) * scale
        logits = logits + c[:, :, lo:hi, None] - c[:, :, None, :hi]
        mask = jnp.arange(hi)[None, :] <= jnp.arange(lo, hi)[:, None]
        p = jax.nn.softmax(jnp.where(mask, logits, -jnp.inf), axis=-1)
        outs.append(jnp.einsum('bhqk,bhkd->bhqd', p.astype(v.dtype), vh[:, :, :hi]))
    return jnp.concatenate(outs, axis=2).transpose(0, 2, 1, 3)

def causal_dwconv(u, w, bias):
    S = u.shape[1]
    up = jnp.pad(u, ((0, 0), (CONV_W - 1, 0), (0, 0)))
    out = bias
    for j in range(CONV_W):
        out = out + w[j] * up[:, j:j + S]
    return out

def hybrid_layer(x, norm_mix_g, w_in, gla_alpha_w2, gla_alpha_b, gla_out_norm_g,
                 fox_forget_b, fox_q_norm_g, fox_k_norm_g, gate_b, w_gla_branch,
                 w_fox_branch, w_out, norm_ffn_g, w_up, conv_w, conv_b, w_down):
    B, S, _ = x.shape
    h = rmsnorm_2(x, norm_mix_g)
    gq, gk, gv, gr, glr, fq, fk, fv, ff, g_gla, g_fox = jnp.split(h @ w_in, IN_OFFSETS, axis=-1)

    log_a = jax.nn.log_sigmoid(glr @ gla_alpha_w2 + gla_alpha_b) / GLA_TAU
    o_gla = gla_chunked(gq.reshape(B, S, GLA_HEADS, GLA_DK) * (GLA_DK ** -0.5),
                        gk.reshape(B, S, GLA_HEADS, GLA_DK),
                        gv.reshape(B, S, GLA_HEADS, GLA_DV),
                        log_a.reshape(B, S, GLA_HEADS, GLA_DK))
    o_gla = rmsnorm_2(o_gla, gla_out_norm_g.reshape(GLA_HEADS, GLA_DV)).reshape(B, S, GLA_WIDTH) * jax.nn.silu(gr)

    fqh = rmsnorm_2(fq.reshape(B, S, FOX_HEADS, FOX_HD), fox_q_norm_g)
    fkh = rmsnorm_2(fk.reshape(B, S, FOX_HEADS, FOX_HD), fox_k_norm_g)
    log_f = jax.nn.log_sigmoid(ff + fox_forget_b)
    o_fox = fox_attention(fqh, fkh, fv.reshape(B, S, FOX_HEADS, FOX_HD), log_f).reshape(B, S, FOX_WIDTH)

    y = jax.nn.sigmoid(g_gla + gate_b[0]) * (o_gla @ w_gla_branch) \
        + jax.nn.sigmoid(g_fox + gate_b[1]) * (o_fox @ w_fox_branch)
    x = x + y @ w_out

    a, val = jnp.split(rmsnorm_2(x, norm_ffn_g) @ w_up, 2, axis=-1)
    a = causal_dwconv(a, conv_w, conv_b)
    return x + (jax.nn.gelu(a) * val) @ w_down

def second_inputs(seed: int = 0) -> dict:
    key = jax.random.key(seed)
    ks = jax.random.split(key, 20)
    L = DEPTH
    nrm = jax.random.normal
    return {
        'x': nrm(ks[0], (BATCH, SEQ, D_MODEL), jnp.float32),
        'norm_mix_g': 1.0 + 0.02 * nrm(ks[1], (L, D_MODEL), jnp.float32),
        'w_in': nrm(ks[2], (L, D_MODEL, IN_COLS_2), jnp.float32) * D_MODEL ** -0.5,
        'gla_alpha_w2': nrm(ks[3], (L, GLA_LOWRANK, GLA_HEADS * GLA_DK), jnp.float32) * GLA_LOWRANK ** -0.5,
        'gla_alpha_b': 0.1 * nrm(ks[4], (L, GLA_HEADS * GLA_DK), jnp.float32),
        'gla_out_norm_g': 1.0 + 0.02 * nrm(ks[5], (L, GLA_WIDTH), jnp.float32),
        'fox_forget_b': 3.0 + nrm(ks[6], (L, FOX_HEADS), jnp.float32),
        'fox_q_norm_g': 1.0 + 0.02 * nrm(ks[7], (L, FOX_HD), jnp.float32),
        'fox_k_norm_g': 1.0 + 0.02 * nrm(ks[8], (L, FOX_HD), jnp.float32),
        'gate_b': 0.1 * nrm(ks[9], (L, 2, D_MODEL), jnp.float32),
        'w_gla_branch': nrm(ks[10], (L, GLA_WIDTH, D_MODEL), jnp.float32) * GLA_WIDTH ** -0.5,
        'w_fox_branch': nrm(ks[11], (L, FOX_WIDTH, D_MODEL), jnp.float32) * FOX_WIDTH ** -0.5,
        'w_out': nrm(ks[12], (L, D_MODEL, D_MODEL), jnp.float32) * D_MODEL ** -0.5,
        'norm_ffn_g': 1.0 + 0.02 * nrm(ks[13], (L, D_MODEL), jnp.float32),
        'w_up': nrm(ks[14], (L, D_MODEL, 2 * D_FF_2), jnp.float32) * D_MODEL ** -0.5,
        'conv_w': nrm(ks[15], (L, CONV_W, D_FF_2), jnp.float32) * CONV_W ** -0.5,
        'conv_b': 0.02 * nrm(ks[16], (L, D_FF_2), jnp.float32),
        'w_down': nrm(ks[17], (L, D_FF_2, D_MODEL), jnp.float32) * D_FF_2 ** -0.5,
        'norm_final_g': 1.0 + 0.02 * nrm(ks[18], (D_MODEL,), jnp.float32),
    }

def second_block(x, norm_mix_g, w_in, gla_alpha_w2, gla_alpha_b, gla_out_norm_g,
              fox_forget_b, fox_q_norm_g, fox_k_norm_g, gate_b, w_gla_branch,
              w_fox_branch, w_out, norm_ffn_g, w_up, conv_w, conv_b, w_down, norm_final_g):
    for l in range(DEPTH):
        x = hybrid_layer(x, norm_mix_g[l], w_in[l], gla_alpha_w2[l], gla_alpha_b[l], gla_out_norm_g[l],
                         fox_forget_b[l], fox_q_norm_g[l], fox_k_norm_g[l], gate_b[l], w_gla_branch[l],
                         w_fox_branch[l], w_out[l], norm_ffn_g[l], w_up[l], conv_w[l], conv_b[l], w_down[l])
    return rmsnorm_2(x, norm_final_g)


def setup_inputs(seed=0):
    out = dict(first_inputs(seed))
    for name, value in second_inputs(seed + 1).items():
        if name != "x":
            out[name + "_2"] = value
    return out


def reference(
    x, c, ctx, c_ctx, w_mod, b_mod, g_pre_mix, g_post_mix, g_pre_ffn, g_post_ffn, w_in, rpb,
    g_qnorm, g_knorm, w_out_a, w_out_b, w_o, w_router, b_router, w_gu, b_gu, w_dn, b_dn,
    norm_mix_g_2, w_in_2, gla_alpha_w2_2, gla_alpha_b_2, gla_out_norm_g_2, fox_forget_b_2,
    fox_q_norm_g_2, fox_k_norm_g_2, gate_b_2, w_gla_branch_2, w_fox_branch_2, w_out_2,
    norm_ffn_g_2, w_up_2, conv_w_2, conv_b_2, w_down_2, norm_final_g_2,
):
    x = first_block(
        x, c, ctx, c_ctx, w_mod, b_mod, g_pre_mix, g_post_mix, g_pre_ffn, g_post_ffn, w_in, rpb,
        g_qnorm, g_knorm, w_out_a, w_out_b, w_o, w_router, b_router, w_gu, b_gu, w_dn, b_dn,
    )
    return second_block(
        x, norm_mix_g_2, w_in_2, gla_alpha_w2_2, gla_alpha_b_2, gla_out_norm_g_2,
        fox_forget_b_2, fox_q_norm_g_2, fox_k_norm_g_2, gate_b_2, w_gla_branch_2,
        w_fox_branch_2, w_out_2, norm_ffn_g_2, w_up_2, conv_w_2, conv_b_2, w_down_2,
        norm_final_g_2,
    )


_drawn_inputs = setup_inputs


def setup_inputs(seed=0):
    import zlib

    import numpy as np

    out = dict(_drawn_inputs(seed))
    spreads = {}
    factors = {'g_post_ffn': 2.977,
     'rpb': 3.609,
     'g_qnorm': 4.543,
     'g_knorm': 4.834,
     'b_router': 2.822,
     'b_gu': 6.633,
     'b_dn': 8.0,
     'norm_mix_g_2': 3.873,
     'gla_alpha_b_2': 3.783,
     'gla_out_norm_g_2': 8.0,
     'fox_q_norm_g_2': 8.0,
     'fox_k_norm_g_2': 8.0,
     'gate_b_2': 3.987,
     'norm_ffn_g_2': 12.512,
     'conv_b_2': 17.303,
     'norm_final_g_2': 7.811}
    for name, (base, spread) in spreads.items():
        noise = np.random.default_rng([zlib.crc32(name.encode()), seed]).standard_normal(out[name].shape)
        drawn = base * np.exp(spread * noise) if base else spread * noise
        out[name] = __import__('jax').numpy.asarray(drawn.astype(out[name].dtype))
    for name, factor in factors.items():
        out[name] = (out[name] * factor).astype(out[name].dtype)
    return out
```

```python
from contextlib import ExitStack

import concourse.bass as bass
import numpy as np
from concourse import mybir

F32 = mybir.dt.float32
I32 = mybir.dt.int32
ALU = mybir.AluOpType
ACT = mybir.ActivationFunctionType
AX = mybir.AxisListType

P = 128
D = 1024
KD = D // P
T = 256
TT = T // P
GRID_W = 64
ROWS = T // GRID_W
DH = 64
NH = 8
NKV = 2
WIN_R, WIN_C = 8, 16
NE = 32
TOPK = 4
CAP = 64
EXTRA = 16
ITEMS = NE + EXTRA
FF2 = 2816
F2T = FF2 // P
RING = 6
SLOT = 4096
EPS = 1e-6
NEG = -1.0e30
SENTINEL = -3.0e38
FAR = 4096.0
CHUNK = 64
NCH = T // CHUNK
TAU = 16.0


def layout(sizes):
    at, out = 0, {}
    for name, n in sizes:
        out[name] = (at, at + n)
        at += n
    return out, at


CONST, CONST_N = layout([
    ("ident", P), ("ones", P), ("tri", TT * T), ("causal", P), ("gla_mask", CHUNK), ("window", GRID_W),
    ("iota", P), ("cos", TT * DH), ("sin", TT * DH), ("carry", T), ("tri32", NE), ("eid", 1), ("eps", 1),
    ("one", 1),
])
COLS, COLS_N = layout([
    ("b_mod", 48), ("g_pre_mix", KD), ("g_post_mix", KD), ("g_pre_ffn", KD), ("g_post_ffn", KD),
    ("norm_mix", KD), ("alpha_b", 2), ("gate_b", 2 * KD), ("norm_ffn", KD), ("conv_w", 3 * F2T),
    ("conv_b", F2T), ("norm_final", KD), ("c", 2 * KD),
])
ROWS_L, ROWS_N = layout([
    ("g_q", DH), ("g_k", DH), ("fox_q", DH), ("fox_k", DH), ("gla_out", 512), ("forget_b", NH), ("b_router", NE),
])


def constants():
    c = np.zeros((P, CONST_N), np.float32)

    def put(name, a):
        lo, hi = CONST[name]
        c[: a.shape[0], lo:hi] = a.reshape(a.shape[0], -1)

    p = np.arange(P)
    t = np.arange(T)
    put("ident", np.eye(P))
    put("ones", np.ones((P, P)))
    s = (np.arange(TT)[None, :] * P + p[:, None])
    put("tri", (s[:, :, None] <= t[None, None, :]).astype(np.float32))
    put("causal", np.where(p[None, :] <= p[:, None], 0.0, NEG))
    put("gla_mask", (p[:, None] % CHUNK <= np.arange(CHUNK)[None, :]).astype(np.float32))
    w = p % GRID_W
    c0 = np.clip(w - WIN_C // 2, 0, GRID_W - WIN_C)
    k = np.arange(GRID_W)
    put("window", np.where((k[None, :] >= c0[:, None]) & (k[None, :] < c0[:, None] + WIN_C), 0.0, NEG))
    put("iota", np.broadcast_to((p % CAP).astype(np.float32), (P, P)))
    nf = DH // 4
    freqs = (np.float32(10000.0) ** (-np.arange(nf, dtype=np.float32) / nf)).astype(np.float32)
    cos, sin = np.zeros((P, TT, DH)), np.zeros((P, TT, DH))
    for blk, pos in enumerate((s // GRID_W, s % GRID_W)):
        ang = pos.astype(np.float32)[:, :, None] * freqs
        at = blk * 2 * nf
        cos[:, :, at:at + nf] = cos[:, :, at + nf:at + 2 * nf] = np.cos(ang)
        sin[:, :, at:at + nf], sin[:, :, at + nf:at + 2 * nf] = -np.sin(ang), np.sin(ang)
    put("cos", cos)
    put("sin", sin)
    put("carry", np.broadcast_to((t % CHUNK != 0).astype(np.float32), (P, T)))
    e = np.arange(NE)
    put("tri32", (e[:, None] <= e[None, :]).astype(np.float32))
    put("eid", e[:, None].astype(np.float32))
    put("eps", np.full((P, 1), EPS))
    put("one", np.ones((P, 1)))
    return c


W_IN_SLOTS = [(0, 512), (512, 1024), (1024, 1280), (1280, 1792), (1792, 2304)] + \
             [(2304 + 512 * i, 2816 + 512 * i) for i in range(4)]
LR0 = 1536
FQ0 = LR0 + 16
FF0 = FQ0 + 3 * 512
G20 = FF0 + NH
W_IN2_SLOTS = [(0, 512), (512, 1024), (1024, 1536), (FQ0, FQ0 + 512), (FQ0 + 512, FQ0 + 1024),
               (FQ0 + 1024, FQ0 + 1536)] + [(G20 + 512 * i, G20 + 512 * (i + 1)) for i in range(4)]

B1_HEAD = 4 + 4 + 2 + 2 + 2
GATE_AFTER = {u: u // 2 for u in range(1, 16, 2)}
BANKS1 = ["act"] * (B1_HEAD + 2 + 4 + 8 + 2) + ["dve"] * 8 + ["act"] * 4
BANKS2 = ["act"] * (12 + 2 + 4 + 8 + 2) + ["dve"] * 8 + ["act"] * 4 + ["dve"] * 22


def two_blocks(nc, A, out):
    with ExitStack() as ctx:
        def sb(name, shape, dt=F32):
            return ctx.enter_context(nc.sbuf_tensor(name, shape, dt))

        def sem(name):
            return ctx.enter_context(nc.semaphore(name))

        ring = sb("ring", [P, RING, SLOT])
        xT = sb("xT", [P, KD, T])
        cst = sb("cst", [P, CONST_N])
        cols = sb("cols", [P, COLS_N])
        rows = sb("rows", [P, ROWS_N])
        ARENA = 17408
        arena = sb("arena", [P, ARENA])
        small = sb("small", [P, 1024])
        table = sb("table", [1, ITEMS + 2], I32)
        PB = [ctx.enter_context(nc.psum_tensor(f"proj{i}", [P, 512], F32)) for i in range(4)]
        AS = [ctx.enter_context(nc.psum_tensor(f"scores{i}", [P, 512], F32)) for i in range(2)]
        PT = ctx.enter_context(nc.psum_tensor("turned", [P, 512], F32))
        AO = ctx.enter_context(nc.psum_tensor("att_out", [P, 512], F32))

        def region(at, *dims, parts=P):
            n = int(np.prod(dims))
            assert at + n <= ARENA
            v = arena[0:parts, at:at + n]
            if len(dims) == 2:
                v = v.rearrange("p (a b) -> p a b", b=dims[1])
            elif len(dims) == 3:
                v = v.rearrange("p (a b c) -> p a b c", b=dims[1], c=dims[2])
            return v

        def C(name):
            lo, hi = CONST[name]
            return cst[:, lo:hi]

        def col(name, i=0, n=1):
            lo, _ = COLS[name]
            return cols[:, lo + i:lo + i + n]

        def row(name):
            lo, hi = ROWS_L[name]
            return rows[:, lo:hi]

        small_at = [0]

        def tiny(n):
            small_at[0] += n
            assert small_at[0] <= 1024
            return small[:, small_at[0] - n:small_at[0]]

        ident, ones = C("ident"), C("ones")
        tri = C("tri").rearrange("p (a t) -> p a t", t=T)

        hT = region(0, KD, T)
        hcT = region(2048, KD, T)
        Pm = region(2048, 2, 512)
        PTs = region(3072, 2, 512)
        bias = region(4096, TT, NH, T)
        gates = region(4096, 2 * KD, T)
        sqx = region(8192, KD, T)
        qaT = region(8192, 4, T)
        kaT = region(9216, 4, 2 * T)
        Va = region(11264, 4, 512)
        ctxT = region(11264, KD, T)
        sqc = region(13312, KD, T)
        qb = region(13312, TT, 512)
        kvb = region(14336, 4, 256)
        otok = region(15360, 512)
        oaT = region(15872, 4, T)
        qbT = region(8192, 4, T)
        kdup = region(9216, 4, 256)
        kbT = region(10240, NKV, 2 * T)
        tmp1 = region(11264, TT, 512)
        tmp2 = region(12288, TT, 512)
        obT = region(12288, 4, T)
        mergedT = region(8192, KD, T)
        yT = region(13312, KD, T)
        sqy = region(2048, KD, T)
        h2tok = region(2048, TT, D)
        bgu = region(4096, 2048)
        bdn = region(6144, D, parts=NE)
        act_t = region(7168, 512)
        OHb = region(7680, CAP)
        logit = region(8192, TT, 40)
        mark = region(8288, TT, 40)
        top8 = region(8384, TT, 8)
        sel = region(8416, TT, NE)
        prob = region(8480, TT, NE)
        posT = region(8544, T, parts=NE)
        wT = region(8800, T, parts=NE)
        OH = region(9056, ITEMS + 1, parts=NE)
        eblk = region(9106, 96, parts=NE)
        wr = region(9216, KD, NE)
        POSI = region(9472, TT, ITEMS + 1)
        WI = region(9600, TT, ITEMS + 1)
        Sel = region(9728, TT, CAP)
        SelW = region(11776 + 512, TT, 2 * CAP)
        SelWT = region(9984, T)
        xe = region(10240, 4, 2, CAP)
        glu = region(10752, 512)
        lin = region(11264, 512)
        esig = region(11776, 512)
        act_s = region(12544, 4, 2, CAP)
        xg = region(13056, 512)
        yb = region(13568, 512)
        sqf = region(14336, KD, T)
        fT = region(10240, KD, T)
        rk1 = region(16896, TT, 128)
        rk2 = region(17152, TT, 128)
        gqk = region(2048, 4, T)
        gv = region(3072, TT, 512)
        gr = region(4096, TT, 512)
        fq = region(5120, TT, 512)
        fk = region(6144, TT, 512)
        fv = region(7168, TT, 512)
        wlr = region(8192, KD, 24)
        aw2 = region(8384, 256, parts=16)
        glrT = region(8640, T, parts=16)
        Z = region(8896, 528)
        Z1 = region(9424, 528)
        bcum = region(9952, 2, T)
        eb = region(10464, 2, T)
        enb = region(10976, 2, T)
        kd = region(11488, 2, T)
        qe = region(12000, 2, T)
        ke = region(12512, 2, T)
        kdtok = region(13024, TT, 256)
        AT = region(13536, TT, 4 * CHUNK)
        St = region(14048, 3, 2, P)
        og = region(14816, TT, 512)
        esr = region(15840, TT, 512)
        fsq = region(10976, TT, 512)
        osq = region(9952, TT, 512)
        otok2 = region(16864, 512)
        ogT = region(2048, 4, T)
        ofT = region(13024, 4, T)
        fqT = region(14816, 4, T)
        fkT = region(15840, 4, T)
        Cb = [region(9952, NH, P), region(10976, NH, T)]
        Pm2 = region(3072, 2, 512)
        PT2 = region(4096, 2, 512)
        gate_spans = [(5120, 8), (8192, 6), (14048, 2)]
        gate_at = [lo + 256 * j for lo, n in gate_spans for j in range(n)]
        gate2_tile = [region(lo, T) for lo in gate_at]
        merged2 = region(3072, KD, T)
        y2T = region(9952, KD, T)
        sq2 = region(12000, KD, T)
        actT = region(2048, F2T, T)
        gf2 = region(7680, 2, 2, T)
        cv2 = region(8704, 2, 2, T)
        ge2 = region(9728, 2, 2, T)

        rstd = tiny(T)
        rstd_c = tiny(T)
        cs = tiny(2 * KD).rearrange("p (k c) -> p k c", c=2)
        cse = tiny(2 * KD).rearrange("p (k c) -> p k c", c=2)
        mod = tiny(96).rearrange("p (k c) -> p k c", c=2)
        A1 = tiny(2 * KD).rearrange("p (k c) -> p k c", c=2)
        A2 = tiny(KD)
        gt1 = tiny(KD)
        gt2 = tiny(KD)
        ssq = tiny(32)
        nmax = tiny(2)
        den = tiny(2 * NH).rearrange("p (t h) -> p t h", h=NH)
        dinv = tiny(NH)
        lsum = tiny(TT)
        linv = tiny(TT)
        nm1 = tiny(TT)
        cq = tiny(TT * NH).rearrange("p (t h) -> p t h", h=NH)
        half_gate_b = tiny(2 * KD)

        landed = [sem(f"slot_landed{i}") for i in range(RING)]
        consts_in = sem("consts_in")
        x_in = sem("x_in")
        ctx_in = sem("ctx_in")
        bias_in = sem("bias_in")
        bias_masked = sem("bias_masked")
        router_in = sem("router_in")
        bgu_in = sem("bgu_in")
        bgu_zeroed = sem("bgu_zeroed")
        small2_in = sem("small2_in")
        out_done = sem("out_done")
        act_step = sem("act_step")
        dve_step = sem("dve_step")
        bank_done = sem("bank_done")
        act_evac = sem("act_evac")
        dve_evac = sem("dve_evac")
        mod_slots = sem("mod_slots_used")
        cs_ready = sem("cs_ready")
        cs_exp = sem("cs_exp")
        mod_ready = sem("mod_ready")
        sq_ready = sem("squares_ready")
        sum_ready = sem("sum_of_squares_ready")
        root_ready = sem("root_ready")
        scaled_ready = sem("scaled_ready")
        h_ready = sem("h_ready")
        scores_ready = sem("scores_ready")
        max_ready = sem("max_ready")
        exp_done = sem("exp_done")
        turned_ready = sem("turned_ready")
        turned_copied = sem("turned_copied")
        pv_done = sem("pv_done")
        att_tile = sem("att_tile_normalised")
        qk_sq = sem("head_squares_ready")
        qk_root = sem("head_root_ready")
        qb_ready = sem("qb_ready")
        merged_ready = sem("merged_ready")
        merged_ready2 = sem("merged_ready_b")
        x_mid = sem("x_mid_ready")
        h2tok_t = sem("h2tok_turned")
        h2tok_c = sem("h2tok_copied")
        route_pe = sem("route_pe")
        route_dve = sem("route_dve")
        route_act = sem("route_act")
        sel_ready = sem("sel_ready")
        gathered = sem("gathered")
        xg_ready = sem("gathered_copied")
        xg_t = sem("gathered_turned")
        xe_ready = sem("xe_ready")
        ohb_ready = sem("expert_onehot_ready")
        bias_added = sem("up_biases_added")
        up_slot = sem("expert_slot_used")
        glu_ready = sem("glu_ready")
        esig_ready = sem("esig_ready")
        actv_ready = sem("activation_ready")
        act_turned = sem("activation_turned")
        act_s_ready = sem("activation_copied")
        selw_ready = sem("selw_ready")
        selwt_t = sem("selw_turned")
        selwt_c = sem("selw_copied")
        yb_c = sem("yb_copied")
        moe_dve = sem("moe_dve_step")
        moe_done = sem("moe_done")
        landed2 = [sem(f"slot_landed_b{i}") for i in range(RING)]
        bank_done2 = sem("bank_done_b")
        act_evac2 = sem("act_evac_b")
        dve_evac2 = sem("dve_evac_b")
        gla_pe = sem("gla_pe")
        gla_dve = sem("gla_dve")
        gla_act = sem("gla_act")
        cb_ready = sem("cb_ready")
        down_slots = sem("down_slots_used")
        ffn_act = sem("ffn_act")
        ffn_gate = sem("ffn_gate")
        actT_ready = sem("actT_ready")
        final_ready = sem("final_ready")

        def w_cols(w, lo, hi):
            return w.rearrange("(k p) n -> p k n", p=P)[:, :, lo:hi]

        stream1 = [w_cols(A["w_mod"], 512 * n, 512 * n + 512) for n in range(12)]
        stream1 += [w_cols(A["w_in"], lo, hi) for lo, hi in W_IN_SLOTS]
        stream1 += [w_cols(A["w_out_a"], 0, D), w_cols(A["w_out_b"], 0, D)]
        stream1 += [w_cols(A["w_o"], 512 * n, 512 * n + 512) for n in range(2)]
        N1 = len(stream1)
        used1 = [(mod_slots, n + 1) for n in range(12)]
        used1 += [(bank_done, v) for v in (4, 8, 10, 12, 14)]
        at = B1_HEAD + 2 + 4
        gate_bank_no = []
        for u in range(16):
            if u == 10:
                at += 1
            if u in GATE_AFTER:
                at += 1
                gate_bank_no.append(at)
        used1 += [(bank_done, gate_bank_no[2 * s + 1]) for s in range(4)]
        M1 = B1_HEAD + 2 + 4 + 8 + 2
        used1 += [(bank_done, M1 + 8)] * 2
        used1 += [(bank_done, M1 + 8 + 2), (bank_done, M1 + 8 + 4)]
        assert len(used1) == N1 and M1 + 12 == len(BANKS1)
        prior = [len([n for n in range(N1) if n % RING == s]) for s in range(RING)]
        last1 = [max(n for n in range(N1) if n % RING == s) for s in range(RING)]

        stream2 = [w_cols(A["w_in_2"], lo, hi) for lo, hi in W_IN2_SLOTS]
        stream2 += [w_cols(A["w_gla"], 0, D), w_cols(A["w_fox"], 0, D)]
        stream2 += [w_cols(A["w_out_2"], 512 * n, 512 * n + 512) for n in range(2)]
        UP0 = len(stream2)
        stream2 += [None] * 11
        DN0 = len(stream2)
        stream2 += [A["w_down"][512 * n:min(512 * n + 512, FF2), :].rearrange("(k p) n -> p k n", p=P)
                    for n in range(6)]
        N2 = len(stream2)
        used2 = [(bank_done2, 2 * n + 2) for n in range(6)]
        at = 12 + 2 + 4
        gate_bank_no2 = []
        for u in range(16):
            if u == 10:
                at += 1
            if u in GATE_AFTER:
                at += 1
                gate_bank_no2.append(at)
        used2 += [(bank_done2, gate_bank_no2[2 * s + 1]) for s in range(4)]
        M2 = 12 + 2 + 4 + 8 + 2
        used2 += [(bank_done2, M2 + 8)] * 2 + [(bank_done2, M2 + 10), (bank_done2, M2 + 12)]
        used2 += [(bank_done2, M2 + 12 + 2 * n + 2) for n in range(11)]
        used2 += [(down_slots, n + 1) for n in range(6)]
        assert len(used2) == N2 and M2 + 12 + 22 == len(BANKS2)

        G1, G2 = B1_HEAD + 2 + 4, 12 + 2 + 4
        out_banks = [B1_HEAD + 1, B1_HEAD + 2, G1 + 6, G1 + 10, G2 + 6, G2 + 10]

        def slot(n, *dims):
            v = ring[:, n % RING, 0:int(np.prod(dims))]
            return v.rearrange("p (k c) -> p k c", c=dims[1])

        def sum_at(k):
            return PB[k // 2][:, (k % 2) * T:(k % 2) * T + T]

        kv_bank, kv_at = [AO, PT, AO], [0, 0, 256]
        c_banks = [AO, AS[0], AO, AS[1]]

        def evacs(banks, upto, who):
            return sum(b == who for b in banks[:upto])

        block = ctx.enter_context(nc.Block())

        @block.sync
        def _(sp):
            def load(n):
                src = stream1[n]
                if n >= RING:
                    sp.wait_ge(*used1[n - RING])
                sp.dma_start(slot(n, src.shape[1], src.shape[2]), src).then_inc(landed[n % RING], 16)

            for n in range(N1):
                load(n)

            def expert(e, s):
                w, n, K, N = (A["w_gu"], s, 2, 2 * D) if s < 4 else (A["w_dn"], s - 4, 4, D)
                src = w[e].rearrange("a (k p) n -> p (a k) n", p=P)[:, K * n:K * n + K, :]
                sp.dma_start(slot(s, K, N), src).then_inc(landed[s], 16)

            for s in range(RING):
                sp.wait_ge(*used1[last1[s]])
                expert(slice(0, 1), s)
            sp.wait_ge(route_dve, 7)
            n_items = sp.value_load(table[0:1, ITEMS:ITEMS + 1], min_val=NE, max_val=ITEMS - 1)
            with sp.Fori(1, n_items) as i:
                e = sp.value_load(table[0:1, bass.ds(i, 1)], min_val=0, max_val=NE - 1)
                for s in range(RING):
                    sp.wait_ge(up_slot, i * RING + (s + 1))
                    expert(bass.ds(e, 1), s)
            for n in range(N2):
                src = stream2[n]
                if n < RING:
                    sp.wait_ge(up_slot, n_items * RING + (n + 1))
                else:
                    sp.wait_ge(*used2[n - RING])
                if UP0 <= n < DN0:
                    for half in range(2):
                        c0 = half * FF2 + 256 * (n - UP0)
                        sp.dma_start(slot(n, KD, 512)[:, :, 256 * half:256 * half + 256],
                                     w_cols(A["w_up"], c0, c0 + 256)).then_inc(landed2[n % RING], 16)
                else:
                    sp.dma_start(slot(n, src.shape[1], src.shape[2]), src).then_inc(landed2[n % RING], 16)
            for c in range(2):
                sp.wait_ge(final_ready, KD // 2 * (c + 1))
                sp.dma_start(out[:, 4 * c:4 * c + 4, :], fT[:, 4 * c:4 * c + 4, :]).then_inc(out_done, 16)
            sp.wait_ge(out_done, 32)

        def land2(n):
            return 16 * sum((2 if UP0 <= m < DN0 else 1) for m in range(n + 1) if m % RING == n % RING)

        @block.gpsimd
        def _(pool):
            pool.wait_ge(bias_in, 16 * ROWS * ROWS)
            pool.wait_ge(consts_in, 48)
            b = bias.rearrange("p t h (r w) -> p (t h r) w", w=GRID_W)
            nc.gpsimd.tensor_tensor(b, b, C("window").unsqueeze(1).to_broadcast([P, TT * NH * ROWS, GRID_W]),
                                    ALU.add).then_inc(bias_masked, 1)

        @block.scalar
        def _(act):
            n_step = [0]

            def step(ins):
                n_step[0] += 1
                ins.then_inc(act_step, 1)
                act.wait_ge(act_step, n_step[0])

            act.dma_start(cst[:], A["cst"]).then_inc(consts_in, 16)
            act.dma_start(cols[:], A["cols"]).then_inc(consts_in, 16)
            act.dma_start(rows[:], A["rows"].partition_broadcast(P)).then_inc(consts_in, 16)
            act.dma_start(xT[:], A["xT"]).then_inc(x_in, 16)
            act.dma_start(ctxT, A["ctxT"]).then_inc(ctx_in, 16)
            for r in range(ROWS):
                half, tt = r % 2, r // 2
                row_at = GRID_W * (2 * GRID_W - 1)
                for r2 in range(ROWS):
                    src = bass.AP(A["rpb"].tensor, A["rpb"].offset + (WIN_R - 1 - r + r2) * row_at + GRID_W - 1,
                                  [[2 * GRID_W - 2, GRID_W], [15 * row_at, NH], [1, GRID_W]])
                    dst = bias[GRID_W * half:GRID_W * half + GRID_W, tt, :, GRID_W * r2:GRID_W * (r2 + 1)]
                    act.dma_start(dst, src).then_inc(bias_in, 16)

            act.wait_ge(consts_in, 48)
            cc = col("c", 0, 2 * KD).rearrange("p (k c) -> p k c", c=2)
            nc.scalar.activation(cse, cc, ACT.Tanh, scale=0.5).then_inc(cs_exp, 1)

            def squares(src, dst):
                nc.scalar.activation(dst, src, ACT.Square).then_inc(sq_ready, 1)

            def root(n, bank, dst):
                act.wait_ge(sum_ready, n)
                nc.scalar.activation(dst, bank[:, 0:T], ACT.Sqrt, scale=1.0 / D, bias=C("eps"))\
                  .then_inc(root_ready, 1)

            act.wait_ge(x_in, 16)
            squares(xT[:], sqx)
            act.wait_ge(ctx_in, 16)
            squares(ctxT, sqc)
            root(1, AS[0], rstd)
            root(2, AS[1], rstd_c)
            act.wait_ge(mod_ready, 1)
            act.wait_ge(scaled_ready, 1)
            for k in range(KD):
                nc.scalar.activation(hT[:, k, :], sqx[:, k, :], ACT.Identity, scale=A1[:, k, 0:1],
                                     bias=mod[:, k, 0:1]).then_inc(h_ready, 1)
            act.wait_ge(scaled_ready, 2)
            for k in range(KD):
                nc.scalar.activation(hcT[:, k, :], sqc[:, k, :], ACT.Identity, scale=A1[:, k, 1:2],
                                     bias=mod[:, k, 1:2]).then_inc(h_ready, 1)

            bank = [0]

            def evac(done, freed, dst, cols_=512, func=ACT.Copy, scale=1.0, view=None, parts=P):
                B = bank[0]
                bank[0] += 1
                act.wait_ge(done, B + 1)
                src = PB[B % 4][0:parts, 0:cols_]
                if view is not None:
                    src = src.rearrange("p (a b) -> p a b", b=view)
                nc.scalar.activation(dst, src, func, scale=scale).then_inc(freed, 1)

            ev1 = lambda dst, *a, **k: evac(bank_done, act_evac, dst, *a, **k)
            for src in range(2):
                for b in range(2):
                    ev1(kaT[:, 2 * b:2 * b + 2, src * T:src * T + T], view=T)
            for i in range(4):
                ev1(Va[:, i, :])
            for i in range(2):
                ev1(kvb[:, 2 * i:2 * i + 2, :], view=256)
            for b in range(2):
                ev1(qaT[:, 2 * b:2 * b + 2, :], view=T, scale=DH ** -0.5)
            for i in range(2):
                ev1(qb[:, i, :])

            def attention(u0, widths, Pb, PTb, done, freed, oT, gate_evac):
                def copy(u):
                    act.wait_ge(turned_ready, u0 + u + 1)
                    if u >= 2:
                        act.wait_ge(pv_done, u0 + u - 1)
                    nc.scalar.activation(PTb[:, u % 2, 0:widths[u]], PT[:, 0:widths[u]], ACT.Copy)\
                      .then_inc(turned_copied, 1)

                for u in range(16):
                    act.wait_ge(max_ready, u0 + u + 1)
                    if u >= 2:
                        act.wait_ge(turned_ready, u0 + u - 1)
                    if u == 0 and u0:
                        act.wait_ge(att_tile, u0 // 8)
                    nc.scalar.activation(Pb[:, u % 2, 0:widths[u]], AS[u % 2][:, 0:widths[u]], ACT.Exp,
                                         bias=nmax[:, u % 2:u % 2 + 1], accum_out=den[:, u // 8, u % 8:u % 8 + 1])\
                      .then_inc(exp_done, 1)
                    if u >= 1:
                        copy(u - 1)
                    if u == 10:
                        evac(done, freed, oT[:, :, 0:P], view=P)
                    if gate_evac and u in GATE_AFTER:
                        gate_evac(GATE_AFTER[u])
                copy(15)
                evac(done, freed, oT[:, :, P:T], view=P)

            attention(0, [512] * 16, Pm, PTs, bank_done, act_evac, oaT, None)
            act.wait_ge(qk_sq, 1)
            nc.scalar.activation(ssq[:, 0:24], ssq[:, 0:24], ACT.Sqrt, scale=1.0 / DH, bias=C("eps"))\
              .then_inc(qk_root, 1)
            for tt in range(TT):
                ev1(qbT[:, :, tt * P:tt * P + P], view=P, scale=DH ** -0.5)
            for g in range(NKV):
                ev1(kbT[:, g, :])

            def gate1(b):
                ev1(gates[:, 2 * b:2 * b + 2, :], view=T, func=ACT.Tanh, scale=0.5)

            attention(16, [512] * 16, Pm, PTs, bank_done, act_evac, obT, gate1)
            bank[0] += 8
            for b in range(4):
                ev1(yT[:, 2 * b:2 * b + 2, :], view=T)
            n_evac1 = evacs(BANKS1, len(BANKS1), "act")
            act.wait_ge(act_evac, n_evac1)
            squares(yT, sqy)
            root(3, AS[0], rstd)
            act.wait_ge(x_mid, KD)
            squares(xT[:], sqy)
            root(4, AS[0], rstd)
            act.wait_ge(scaled_ready, 3)
            for k in range(KD):
                nc.scalar.activation(hT[:, k, :], sqy[:, k, :], ACT.Identity, scale=A2[:, k:k + 1],
                                     bias=mod[:, 24 + k, 0:1]).then_inc(h_ready, 1)
            act.wait_ge(bgu_zeroed, 1)
            act.dma_start(bgu[0:NE, :], A["b_gu"]).then_inc(bgu_in, 16)
            act.dma_start(bdn, A["b_dn"]).then_inc(bgu_in, 16)
            act.dma_start(wr, A["w_router"].rearrange("(k p) n -> p k n", p=P)).then_inc(router_in, 16)
            for c in range(4):
                act.wait_ge(h2tok_t, c + 1)
                nc.scalar.activation(h2tok[:, c // 2, 512 * (c % 2):512 * (c % 2) + 512], PB[c][:, :], ACT.Copy)\
                  .then_inc(h2tok_c, 1)
            act.wait_ge(route_dve, 1)
            for tt in range(TT):
                nc.scalar.activation(prob[:, tt, :], logit[:, tt, 0:NE], ACT.Exp, bias=nm1[:, tt:tt + 1])\
                  .then_inc(route_act, 1)
            act.wait_ge(xg_t, 1)
            nc.scalar.activation(xe.rearrange("p a h c -> p (a h c)"), AO[:, :], ACT.Copy).then_inc(xe_ready, 1)
            act.wait_ge(route_dve, 7)
            n_items = act.value_load(table[0:1, ITEMS:ITEMS + 1], min_val=NE, max_val=ITEMS - 1)
            with act.Fori(0, n_items) as i:
                act.wait_ge(xg_t, i + 2)
                nc.scalar.activation(xe.rearrange("p a h c -> p (a h c)"), AO[:, :], ACT.Copy).then_inc(xe_ready, 1)
                act.wait_ge(glu_ready, i + 1)
                nc.scalar.activation(esig, glu, ACT.Tanh, scale=0.5 * 1.702).then_inc(esig_ready, 1)
                act.wait_ge(act_turned, i + 1)
                nc.scalar.activation(act_s.rearrange("p a h c -> p (a h c)"), PT[:, :], ACT.Copy)\
                  .then_inc(act_s_ready, 1)
                act.wait_ge(selwt_t, i + 1)
                nc.scalar.activation(SelWT, PT[:, 0:T], ACT.Copy).then_inc(selwt_c, 1)
                act.wait_ge(up_slot, i * RING + 2 * RING)
                nc.scalar.activation(yb, AO[:, :], ACT.Copy, scale=0.5).then_inc(yb_c, 1)
            act.wait_ge(moe_done, 1)
            for k in range(KD):
                nc.scalar.activation(sqf[:, k, :], sum_at(k), ACT.Square)
                ins = nc.scalar.activation(fT[:, k, :], sum_at(k), ACT.Copy)
            ins.then_inc(sq_ready, 1)
            root(5, AS[0], rstd)
            act.wait_ge(x_mid, 2 * KD)
            squares(xT[:], sqf)
            root(6, AS[0], rstd)

            act.dma_start(wlr[:, :, 0:16], w_cols(A["w_in_2"], LR0, LR0 + 16),
                          allow_slow_non_contiguous=True).then_inc(small2_in, 16)
            act.dma_start(wlr[:, :, 16:24], w_cols(A["w_in_2"], FF0, FF0 + NH),
                          allow_slow_non_contiguous=True).then_inc(small2_in, 16)
            act.dma_start(aw2, A["alpha_w2"]).then_inc(small2_in, 16)
            bank[0] = 0
            ev2 = lambda dst, *a, **k: evac(bank_done2, act_evac2, dst, *a, **k)
            act.wait_ge(gla_pe, 1)
            nc.scalar.activation(glrT, PT[0:16, 0:T], ACT.Copy).then_inc(gla_act, 1)
            act.wait_ge(gla_pe, 3)
            for j in range(2):
                nc.scalar.activation(Z[:, j * T:j * T + T], AO[:, j * T:j * T + T], ACT.Identity,
                                     bias=col("alpha_b", j)).then_inc(gla_act, 1)
            act.wait_ge(gla_dve, 1)
            step(nc.scalar.activation(Z1, Z1, ACT.Exp, scale=-1.0))
            nc.scalar.activation(Z1, Z1, ACT.Ln, bias=C("one")).then_inc(gla_act, 1)
            for b in range(2):
                ev2(gqk[:, 2 * b:2 * b + 2, :], view=T)
            act.wait_ge(gla_dve, 2)
            nc.scalar.activation(eb, bcum, ACT.Exp).then_inc(gla_act, 1)
            nc.scalar.activation(enb, bcum, ACT.Exp, scale=-1.0).then_inc(gla_act, 1)
            nc.scalar.activation(kd, kd, ACT.Exp).then_inc(gla_act, 1)
            for dst in (gv, gr, fq, fk, fv):
                for tt in range(TT):
                    ev2(dst[:, tt, :])
                if dst is gr:
                    act.wait_ge(act_evac2, 6)
                    nc.scalar.activation(esr, gr, ACT.Tanh, scale=0.5).then_inc(gla_act, 1)
            act.wait_ge(gla_pe, 5)
            nc.scalar.activation(kdtok, PT[:, :].rearrange("p (a b) -> p a b", b=256), ACT.Copy)\
              .then_inc(gla_act, 1)
            act.wait_ge(qk_sq, 2)
            nc.scalar.activation(ssq[:, 0:32], ssq[:, 0:32], ACT.Sqrt, scale=1.0 / DH, bias=C("eps"))\
              .then_inc(qk_root, 1)
            act.wait_ge(gla_pe, 8)
            og5 = og.rearrange("p t (a b v) -> p t a b v", b=2, v=P)
            for odd, src in enumerate((AO, PT)):
                nc.scalar.activation(og5[CHUNK:P, 0, :, odd, :],
                                     src[CHUNK:P, 0:256].rearrange("p (a v) -> p a v", v=P), ACT.Copy)
                ins = nc.scalar.activation(og5[:, 1, :, odd, :], src[:, 256:512].rearrange("p (a v) -> p a v", v=P),
                                           ACT.Copy)
            ins.then_inc(gla_act, 1)
            act.wait_ge(gla_dve, 6)
            nc.scalar.activation(osq, og, ACT.Square).then_inc(gla_act, 1)
            act.wait_ge(gla_dve, 7)
            nc.scalar.activation(den[:, 0, :], den[:, 0, :], ACT.Sqrt, scale=1.0 / P, bias=C("eps"))\
              .then_inc(gla_act, 1)
            for tt in range(TT):
                ev2(ogT[:, :, tt * P:tt * P + P], view=P)
            for tt in range(TT):
                ev2(fqT[:, :, tt * P:tt * P + P], view=P, scale=DH ** -0.5)
                ev2(fkT[:, :, tt * P:tt * P + P], view=P)
            def gate2(b):
                B = bank[0]
                bank[0] += 1
                act.wait_ge(bank_done2, B + 1)
                for j in range(2):
                    ins = nc.scalar.activation(gate2_tile[2 * b + j], PB[B % 4][:, j * T:j * T + T], ACT.Tanh,
                                               scale=0.5, bias=half_gate_b[:, 2 * b + j:2 * b + j + 1])
                ins.then_inc(act_evac2, 1)

            attention(32, [P] * 8 + [T] * 8, Pm2, PT2, bank_done2, act_evac2, ofT, gate2)
            bank[0] += 8
            for b in range(4):
                ev2(y2T[:, 2 * b:2 * b + 2, :], view=T)
            act.wait_ge(x_mid, 3 * KD)
            squares(xT[:], sq2)
            root(7, AS[0], rstd)
            for s in range(11):
                cv, ge = cv2[:, s % 2], ge2[:, s % 2]
                if s >= 2:
                    act.wait_ge(actT_ready, s - 1)
                act.wait_ge(ffn_gate, 2 * s + 1)
                nc.scalar.activation(ge, cv, ACT.Square).then_inc(ffn_act, 1)
                act.wait_ge(ffn_gate, 2 * s + 2)
                nc.scalar.activation(ge, ge, ACT.Tanh, scale=0.7978845608028654).then_inc(ffn_act, 1)
            act.wait_ge(x_mid, 4 * KD)
            squares(xT[:], sq2)
            root(8, AS[0], rstd)

        @block.vector
        def _(dve):
            V = nc.vector
            n_step = [0]

            def step(ins):
                n_step[0] += 1
                ins.then_inc(dve_step, 1)
                dve.wait_ge(dve_step, n_step[0])

            def bc(ap, n, mid=True):
                return ap.unsqueeze(1).to_broadcast([P, n, ap.shape[-1]]) if mid else \
                    ap.unsqueeze(2).to_broadcast([P, ap.shape[-1], n])

            def scale_rows(src, dst, n, r):
                dve.wait_ge(root_ready, n)
                step(V.reciprocal(r, r))
                return V.tensor_tensor(dst, src, bc(r, KD), ALU.mult)

            cc = col("c", 0, 2 * KD).rearrange("p (k c) -> p k c", c=2)
            dve.wait_ge(consts_in, 48)
            dve.wait_ge(cs_exp, 1)
            step(V.tensor_scalar(cse, cse, 0.5, 0.5, ALU.mult, ALU.add))
            V.tensor_tensor(cs, cc, cse, ALU.mult).then_inc(cs_ready, 1)
            dve.wait_ge(x_in, 16)
            scale_rows(xT[:], sqx, 1, rstd).then_inc(scaled_ready, 1)
            dve.wait_ge(ctx_in, 16)
            scale_rows(ctxT, sqc, 2, rstd_c).then_inc(scaled_ready, 1)
            dve.wait_ge(mod_slots, 12)
            step(V.tensor_tensor(mod, PT[:, 0:96].rearrange("p (k c) -> p k c", c=2),
                                 bc(col("b_mod", 0, 48), 2, mid=False), ALU.add))
            V.scalar_tensor_tensor(out=A1, in0=mod[:, 8:16, :], scalar=1.0,
                                   in1=bc(col("g_pre_mix", 0, 8), 2, mid=False), op0=ALU.add, op1=ALU.mult)
            V.scalar_tensor_tensor(out=A2, in0=mod[:, 32:40, 0], scalar=1.0, in1=col("g_pre_ffn", 0, 8),
                                   op0=ALU.add, op1=ALU.mult)
            V.tensor_tensor(gt1, mod[:, 16:24, 0], col("g_post_mix", 0, 8), ALU.mult)
            V.tensor_tensor(gt2, mod[:, 40:48, 0], col("g_post_ffn", 0, 8), ALU.mult).then_inc(mod_ready, 1)

            def attention(u0, widths, bias_of, ot):
                def finish(tile):
                    dve.wait_ge(exp_done, u0 + 8 * tile + 8)
                    dve.wait_ge(pv_done, u0 + 8 * tile + 8)
                    step(V.reciprocal(dinv, den[:, tile, :]))
                    g = u0 // 8 + tile
                    if g not in (0, 4):
                        dve.wait_ge(bank_done if u0 < 32 else bank_done2, out_banks[g - 1])
                    V.tensor_tensor(ot.rearrange("p (h d) -> p h d", d=DH),
                                    AO[:, :].rearrange("p (h d) -> p h d", d=DH),
                                    bc(dinv, DH, mid=False), ALU.mult).then_inc(att_tile, 1)

                for u in range(16):
                    w = widths[u]
                    dve.wait_ge(scores_ready, u0 + u + 1)
                    if bias_of(u) is not None:
                        b = bias_of(u)
                        step(V.tensor_tensor(AS[u % 2][:, 0:b.shape[-1]], AS[u % 2][:, 0:b.shape[-1]], b, ALU.add))
                    if u >= 2:
                        dve.wait_ge(exp_done, u0 + u - 1)
                    step(V.reduce_max(nmax[:, u % 2:u % 2 + 1], AS[u % 2][:, 0:w], AX.X))
                    V.tensor_scalar(nmax[:, u % 2:u % 2 + 1], nmax[:, u % 2:u % 2 + 1], -1.0, None, ALU.mult)\
                     .then_inc(max_ready, 1)
                    if u == 9:
                        finish(0)
                finish(1)

            dve.wait_ge(bias_masked, 1)
            attention(0, [512] * 16, lambda u: bias[:, u // 8, u % 8, :], otok)

            q3 = qb.rearrange("p t (h d) -> p (t h) d", d=DH)
            k4 = kvb[:, :, 0:128]
            t1q = tmp1.rearrange("p t (h d) -> p (t h) d", d=DH)
            t2k = tmp2.rearrange("p t c -> p (t c)")[:, 0:512].rearrange("p (t c) -> p t c", c=128)
            dve.wait_ge(pv_done, 16)
            dve.wait_ge(act_evac, B1_HEAD)
            V.tensor_tensor(t1q, q3, q3, ALU.mult)
            step(V.tensor_tensor(t2k, k4, k4, ALU.mult))
            V.reduce_sum(ssq[:, 0:16], t1q, AX.X)
            V.reduce_sum(ssq[:, 16:24], t2k.rearrange("p t (g d) -> p t g d", d=DH), AX.X).then_inc(qk_sq, 1)
            dve.wait_ge(qk_root, 1)
            step(V.reciprocal(ssq[:, 0:24], ssq[:, 0:24]))
            V.tensor_tensor(q3, q3, bc(ssq[:, 0:16], DH, mid=False), ALU.mult)
            for i in range(4):
                ins = V.tensor_tensor(k4[:, i, :].rearrange("p (g d) -> p g d", d=DH),
                                      k4[:, i, :].rearrange("p (g d) -> p g d", d=DH),
                                      bc(ssq[:, 16 + 2 * i:18 + 2 * i], DH, mid=False), ALU.mult)
            step(ins)
            V.tensor_tensor(q3, q3, bc(row("g_q"), 16), ALU.mult)
            for i in range(4):
                ins = V.tensor_tensor(k4[:, i, :].rearrange("p (g d) -> p g d", d=DH),
                                      k4[:, i, :].rearrange("p (g d) -> p g d", d=DH), bc(row("g_k"), NKV), ALU.mult)
            step(ins)
            cos = C("cos").rearrange("p (t d) -> p t d", d=DH)
            sin = C("sin").rearrange("p (t d) -> p t d", d=DH)
            for tt in range(TT):
                for src, n, a, b in ((qb[:, tt, :], NH, tmp1[:, tt, :], tmp2[:, tt, :]),
                                     (kvb[:, tt, 0:128], NKV, rk1[:, tt, :], rk2[:, tt, :])):
                    V.tensor_tensor(a.rearrange("p (h d) -> p h d", d=DH), src.rearrange("p (h d) -> p h d", d=DH),
                                    bc(cos[:, tt, :], n), ALU.mult)
                    for half in range(2):
                        s4 = src.rearrange("p (g b f) -> p g b f", b=2, f=16)[:, :, 1 - half, :]
                        o4 = b.rearrange("p (g b f) -> p g b f", b=2, f=16)[:, :, half, :]
                        s3 = sin[:, tt, :].rearrange("p (g b f) -> p g b f", b=2, f=16)[:, :, half, :]
                        s4 = s4.rearrange("p (h g) f -> p h g f", g=2)
                        o4 = o4.rearrange("p (h g) f -> p h g f", g=2)
                        ins = V.tensor_tensor(o4, s4, s3.unsqueeze(1).to_broadcast([P, n, 2, 16]), ALU.mult)
            step(ins)
            V.tensor_tensor(qb, tmp1, tmp2, ALU.add)
            step(V.tensor_tensor(kvb[:, 0:2, 0:128], rk1, rk2, ALU.add))
            for i in range(4):
                for u in range(2):
                    ins = V.tensor_copy(kdup[:, i, :].rearrange("p (g u d) -> p g u d", u=2, d=DH)[:, :, u, :],
                                        k4[:, i, :].rearrange("p (g d) -> p g d", d=DH))
            ins.then_inc(qb_ready, 1)
            attention(16, [512] * 16, lambda u: None, otok)

            def sigmoid_gates(g):
                step(V.tensor_scalar(g, g, 0.5, 0.5, ALU.mult, ALU.add))

            def merge(B0, done, freed, ga, gb, dst, ready):
                for j in range(KD):
                    B = B0 + j
                    dve.wait_ge(done, B + 1)
                    V.tensor_tensor(ga(j), ga(j), PB[B % 4][:, 0:T], ALU.mult)
                    V.tensor_tensor(gb(j), gb(j), PB[B % 4][:, T:2 * T], ALU.mult).then_inc(freed, 1)
                    dve.wait_ge(freed, j + 1)
                    V.tensor_tensor(dst[:, j, :], ga(j), gb(j), ALU.add).then_inc(ready, 1)

            dve.wait_ge(act_evac, evacs(BANKS1, M1, "act"))
            sigmoid_gates(gates)
            merge(M1, bank_done, dve_evac, lambda j: gates[:, j, :], lambda j: gates[:, KD + j, :],
                  mergedT, merged_ready)

            def add_to_x(src, gain):
                for k in range(KD):
                    ins = V.scalar_tensor_tensor(out=xT[:, k, :], in0=src[:, k, :], scalar=gain(k),
                                                 in1=xT[:, k, :], op0=ALU.mult, op1=ALU.add)
                    ins.then_inc(x_mid, 1)

            dve.wait_ge(act_evac, evacs(BANKS1, len(BANKS1), "act"))
            step(scale_rows(yT, yT, 3, rstd))
            add_to_x(yT, lambda k: gt1[:, k:k + 1])
            dve.wait_ge(x_mid, KD)
            scale_rows(xT[:], sqy, 4, rstd).then_inc(scaled_ready, 1)

            V.memset(bgu, 0.0).then_inc(bgu_zeroed, 1)
            V.memset(OHb, 0.0)
            V.memset(logit, SENTINEL)
            V.memset(POSI, -FAR)
            step(V.memset(WI, 0.0))
            dve.wait_ge(route_pe, 1)
            step(V.tensor_tensor(logit[:, :, 0:NE], AS[0][:, 0:TT * NE].rearrange("p (t e) -> p t e", e=NE),
                                 bc(row("b_router"), TT), ALU.add))
            for tt in range(TT):
                ins = V.max(top8[:, tt, :], logit[:, tt, 0:NE])
            step(ins)
            V.tensor_scalar(nm1, top8[:, :, 0], -1.0, None, ALU.mult).then_inc(route_dve, 1)
            step(V.memset(top8[:, :, TOPK:8], SENTINEL))
            for tt in range(TT):
                ins = V.match_replace(mark[:, tt, :], top8[:, tt, :], logit[:, tt, :], 3.0e38)
            step(ins)
            step(V.tensor_tensor(sel, mark[:, :, 0:NE], logit[:, :, 0:NE], ALU.is_gt))
            dve.wait_ge(route_act, 2)
            step(V.tensor_tensor(prob, prob, sel, ALU.mult))
            step(V.reduce_sum(lsum, prob, AX.X))
            step(V.reciprocal(linv, lsum))
            V.tensor_tensor(WI[:, :, 0:NE], prob, bc(linv, NE, mid=False), ALU.mult).then_inc(route_dve, 1)
            dve.wait_ge(route_dve, 2)
            dve.wait_ge(route_pe, 2)
            step(V.tensor_scalar(mark[:, :, 0:NE], sel, FAR, -FAR - 1.0, ALU.mult, ALU.add))
            V.tensor_tensor(POSI[:, :, 0:NE], mark[:, :, 0:NE],
                            AS[1][:, 0:TT * NE].rearrange("p (t e) -> p t e", e=NE), ALU.add)\
             .then_inc(route_dve, 1)
            n_e = eblk[:, 0:1]
            nov = eblk[:, 1:2]
            step(V.tensor_copy(n_e, AO[0:NE, 0:1]))
            step(V.tensor_scalar(nov, n_e, float(CAP), None, ALU.is_gt))
            for m in range(2, T // CAP):
                step(V.scalar_tensor_tensor(out=nov, in0=n_e, scalar=float(m * CAP), in1=nov, op0=ALU.is_gt,
                                            op1=ALU.add))
            V.tensor_copy(eblk[:, 2:3], nov).then_inc(route_dve, 1)
            dve.wait_ge(route_pe, 3)
            ov_end, ov_start = eblk[:, 3:4], eblk[:, 4:5]
            step(V.tensor_copy(ov_end, AO[0:NE, 1:2]))
            step(V.tensor_tensor(ov_start, ov_end, nov, ALU.subtract))
            io = C("iota")[0:NE, 0:EXTRA]
            g1, g2, jj = eblk[:, 16:32], eblk[:, 32:48], eblk[:, 48:64]
            V.memset(OH[:, ITEMS:ITEMS + 1], 0.0)
            V.tensor_copy(OH[:, 0:NE], ident[0:NE, 0:NE])
            step(V.tensor_scalar(g1, io, ov_start, None, ALU.is_ge))
            step(V.scalar_tensor_tensor(out=OH[:, NE:ITEMS], in0=io, scalar=ov_end, in1=g1, op0=ALU.is_lt,
                                        op1=ALU.mult))
            step(V.tensor_scalar(g2, io, ov_start, 1.0, ALU.subtract, ALU.add))
            step(V.tensor_tensor(jj, g2, OH[:, NE:ITEMS], ALU.mult))
            V.tensor_scalar(jj, jj, -float(CAP), None, ALU.mult).then_inc(route_dve, 1)
            dve.wait_ge(route_pe, 4)
            V.tensor_copy(posT, PT[0:NE, 0:T])
            V.tensor_copy(wT, PT[0:NE, T:2 * T]).then_inc(route_dve, 1)
            dve.wait_ge(route_pe, 6)
            V.tensor_copy(POSI[:, :, NE:ITEMS], AO[:, 8:8 + TT * EXTRA].rearrange("p (t e) -> p t e", e=EXTRA))
            V.tensor_copy(WI[:, :, NE:ITEMS], AO[:, 64:64 + TT * EXTRA].rearrange("p (t e) -> p t e", e=EXTRA))
            V.tensor_copy(table[0:1, 0:NE], C("iota")[0:1, 0:NE])
            V.tensor_copy(table[0:1, NE:ITEMS], AO[0:1, 128:128 + EXTRA])
            V.tensor_scalar(table[0:1, ITEMS:ITEMS + 1], AO[0:1, 160:161], float(NE), None, ALU.add)
            V.memset(SelWT, 0.0).then_inc(selwt_c, 1)
            V.memset(SelW, 0.0).then_inc(route_dve, 1)
            V.memset(yb, 0.0).then_inc(yb_c, 1)
            dve.wait_ge(route_dve, 7)

            def one_hots(at):
                for tt in range(TT):
                    ins = V.tensor_scalar(Sel[:, tt, :], C("iota")[:, 0:CAP], POSI[:, tt, at], None, ALU.is_equal)
                ins.then_inc(sel_ready, 1)

            def weighted_one_hots(at):
                for tt in range(TT):
                    ins = V.tensor_scalar(SelW[:, tt, :], C("iota"), POSI[:, tt, at], WI[:, tt, at],
                                          ALU.is_equal, ALU.mult)
                ins.then_inc(selw_ready, 1)

            def expert_one_hot(at):
                V.tensor_copy(OHb[0:NE, :], OH[:, at].to_broadcast([NE, CAP])).then_inc(ohb_ready, 1)

            one_hots(slice(0, 1))
            expert_one_hot(slice(0, 1))
            weighted_one_hots(slice(0, 1))
            dve.wait_ge(gathered, 1)
            V.tensor_copy(xg, PT[:, :]).then_inc(xg_ready, 1)
            n_items = dve.value_load(table[0:1, ITEMS:ITEMS + 1], min_val=NE, max_val=ITEMS - 1)
            with dve.Fori(0, n_items) as i:
                STEPS = 2
                k_step = [0]

                def mstep(ins):
                    k_step[0] += 1
                    ins.then_inc(moe_dve, 1)
                    dve.wait_ge(moe_dve, i * STEPS + k_step[0])

                dve.wait_ge(gathered, i + 1)
                one_hots(bass.ds(i + 1, 1))
                dve.wait_ge(bias_added, i + 1)
                expert_one_hot(bass.ds(i + 1, 1))
                dve.wait_ge(xg_t, i + 1)
                dve.wait_ge(gathered, i + 2)
                V.tensor_copy(xg, PT[:, :]).then_inc(xg_ready, 1)
                dve.wait_ge(up_slot, i * RING + (RING + 4))
                V.tensor_scalar(glu, AS[0][:, :], 7.0, None, ALU.min).then_inc(glu_ready, 1)
                mstep(V.tensor_scalar(lin, AS[1][:, :], 7.0, -7.0, ALU.min, ALU.max))
                dve.wait_ge(glu_ready, i + 1)
                mstep(V.scalar_tensor_tensor(out=lin, in0=lin, scalar=1.0, in1=glu, op0=ALU.add, op1=ALU.mult))
                dve.wait_ge(esig_ready, i + 1)
                V.scalar_tensor_tensor(out=act_t, in0=esig, scalar=1.0, in1=lin, op0=ALU.add, op1=ALU.mult)\
                 .then_inc(actv_ready, 1)
                dve.wait_ge(selwt_t, i + 1)
                weighted_one_hots(bass.ds(i + 1, 1))

            dve.wait_ge(moe_done, 1)
            dve.wait_ge(sq_ready, 5)
            step(scale_rows(fT, fT, 5, rstd))
            add_to_x(fT, lambda k: gt2[:, k:k + 1])
            dve.wait_ge(x_mid, 2 * KD)

            def norm_x(n, gain):
                dve.wait_ge(root_ready, n)
                step(V.reciprocal(rstd, rstd))
                for k in range(KD):
                    V.scalar_tensor_tensor(out=hT[:, k, :], in0=xT[:, k, :], scalar=col(gain, k), in1=rstd,
                                           op0=ALU.mult, op1=ALU.mult).then_inc(h_ready, 1)

            norm_x(6, "norm_mix")
            V.tensor_scalar(half_gate_b, col("gate_b", 0, 2 * KD), 0.5, None, ALU.mult)
            dve.wait_ge(gla_act, 3)
            dve.wait_ge(gla_pe, 3)
            step(V.tensor_tensor(Z[:, 512:528].rearrange("p (t h) -> p t h", h=NH),
                                 AS[1][:, 0:16].rearrange("p (t h) -> p t h", h=NH), bc(row("forget_b"), TT), ALU.add))
            V.scalar_tensor_tensor(out=Z1, in0=Z, scalar=-1.0, in1=Z, op0=ALU.mult, op1=ALU.max).then_inc(gla_dve, 1)
            dve.wait_ge(gla_act, 4)
            step(V.scalar_tensor_tensor(out=Z, in0=Z, scalar=0.0, in1=Z1, op0=ALU.min, op1=ALU.subtract))
            step(V.tensor_scalar(Z[:, 0:512], Z[:, 0:512], 1.0 / TAU, None, ALU.mult))
            for j in range(2):
                ins = V.tensor_tensor_scan(bcum[:, j, :], C("carry"), Z[:, j * T:j * T + T], 0.0, ALU.mult, ALU.add)
            step(ins)
            b4 = bcum.rearrange("p j (n l) -> p (j n) l", l=CHUNK)
            V.tensor_tensor(kd.rearrange("p j (n l) -> p (j n) l", l=CHUNK),
                            b4[:, :, CHUNK - 1:CHUNK].to_broadcast([P, 2 * NCH, CHUNK]), b4, ALU.subtract)\
             .then_inc(gla_dve, 1)
            dve.wait_ge(gla_act, 7)
            dve.wait_ge(act_evac2, 2)
            V.scalar_tensor_tensor(out=qe, in0=gqk[:, 0:2, :], scalar=DH ** -0.5, in1=eb, op0=ALU.mult, op1=ALU.mult)
            V.tensor_tensor(ke, gqk[:, 2:4, :], enb, ALU.mult)
            V.tensor_tensor(kd, gqk[:, 2:4, :], kd, ALU.mult).then_inc(gla_dve, 1)
            dve.wait_ge(gla_pe, 4)
            for odd in range(2):
                ins = V.tensor_tensor(AT.rearrange("p t (a b l) -> p (t a) b l", b=2, l=CHUNK)[:, :, odd, :],
                                      AS[odd][:, 0:256].rearrange("p (a l) -> p a l", l=CHUNK),
                                      C("gla_mask").unsqueeze(1).to_broadcast([P, TT * 2, CHUNK]), ALU.mult)
            ins.then_inc(gla_dve, 1)
            dve.wait_ge(gla_pe, 7)
            kv = lambda n: kv_bank[n][:, kv_at[n]:kv_at[n] + 256].rearrange("p (j v) -> p j v", v=P)
            step(V.tensor_copy(St[:, 0], kv(0)))
            for n in range(1, 3):
                for j in range(2):
                    ins = V.scalar_tensor_tensor(out=St[:, n, j, :], in0=St[:, n - 1, j, :],
                                                 scalar=eb[:, j, CHUNK * n + CHUNK - 1:CHUNK * n + CHUNK],
                                                 in1=kv(n)[:, j, :], op0=ALU.mult, op1=ALU.add)
                if n < 2:
                    step(ins)
                else:
                    ins.then_inc(gla_dve, 1)
            dve.wait_ge(gla_act, 8)
            step(V.tensor_scalar(esr, esr, 0.5, 0.5, ALU.mult, ALU.add))
            step(V.tensor_tensor(esr, esr, gr, ALU.mult))
            step(V.tensor_tensor(esr, esr, bc(row("gla_out"), TT), ALU.mult))
            dve.wait_ge(act_evac2, 12)
            for src, at in ((fq, 0), (fk, 16)):
                s3 = src.rearrange("p t (h d) -> p (t h) d", d=DH)
                f3 = fsq.rearrange("p t (h d) -> p (t h) d", d=DH)
                step(V.tensor_tensor(f3, s3, s3, ALU.mult))
                ins = V.reduce_sum(ssq[:, at:at + 16], f3, AX.X)
                if at == 0:
                    step(ins)
            ins.then_inc(qk_sq, 1)
            dve.wait_ge(gla_act, 10)
            V.tensor_copy(og[0:CHUNK, 0, :], AS[0][0:CHUNK, :])
            V.tensor_tensor(og[CHUNK:P, 0, :], og[CHUNK:P, 0, :], AS[0][CHUNK:P, :], ALU.add)
            V.tensor_tensor(og[:, 1, :], og[:, 1, :], AS[1][:, :], ALU.add).then_inc(gla_dve, 1)
            dve.wait_ge(gla_act, 11)
            V.reduce_sum(den[:, 0, :], osq.rearrange("p t (h v) -> p (t h) v", v=P), AX.X).then_inc(gla_dve, 1)
            dve.wait_ge(gla_act, 12)
            step(V.reciprocal(dinv, den[:, 0, :]))
            o3 = og.rearrange("p t (h v) -> p (t h) v", v=P)
            step(V.tensor_tensor(o3, o3, bc(dinv, P, mid=False), ALU.mult))
            V.tensor_tensor(og, og, esr, ALU.mult).then_inc(gla_dve, 1)
            dve.wait_ge(qk_root, 2)
            step(V.reciprocal(ssq[:, 0:32], ssq[:, 0:32]))
            for src, at in ((fq, 0), (fk, 16)):
                s3 = src.rearrange("p t (h d) -> p (t h) d", d=DH)
                ins = V.tensor_tensor(s3, s3, bc(ssq[:, at:at + 16], DH, mid=False), ALU.mult)
            step(ins)
            for src, gain in ((fq, "fox_q"), (fk, "fox_k")):
                s3 = src.rearrange("p t (h d) -> p (t h) d", d=DH)
                ins = V.tensor_tensor(s3, s3, bc(row(gain), 16), ALU.mult)
            ins.then_inc(qb_ready, 1)
            dve.wait_ge(gla_pe, 9)
            step(V.tensor_copy(cq, PT[:, 0:TT * NH].rearrange("p (t h) -> p t h", h=NH)))
            for pair in range(4):
                dve.wait_ge(gla_pe, 10 + pair)
                bankp = c_banks[pair]
                for hh in range(2):
                    h = 2 * pair + hh
                    for tt in range(TT):
                        n = P * (tt + 1)
                        ins = V.tensor_scalar(Cb[tt][:, h, :], bankp[:, hh * T:hh * T + n], -1.0, cq[:, tt, h:h + 1],
                                              ALU.mult, ALU.add)
                ins.then_inc(cb_ready, 1)
            dve.wait_ge(cb_ready, 4)
            for tt in range(TT):
                ins = V.tensor_tensor(Cb[tt][:, :, P * tt:P * tt + P], Cb[tt][:, :, P * tt:P * tt + P],
                                      bc(C("causal"), NH), ALU.add)
            step(ins)
            attention(32, [P] * 8 + [T] * 8, lambda u: Cb[u // 8][:, u % 8, :], otok2)

            dve.wait_ge(act_evac2, evacs(BANKS2, M2, "act"))
            for lo, n in gate_spans:
                sigmoid_gates(region(lo, 256 * n))
            merge(M2, bank_done2, dve_evac2, lambda j: gate2_tile[j], lambda j: gate2_tile[KD + j], merged2,
                  merged_ready2)
            dve.wait_ge(act_evac2, evacs(BANKS2, len(BANKS2), "act"))
            for k in range(KD):
                V.tensor_tensor(xT[:, k, :], xT[:, k, :], y2T[:, k, :], ALU.add).then_inc(x_mid, 1)
            dve.wait_ge(x_mid, 3 * KD)
            norm_x(7, "norm_ffn")

            for s in range(11):
                B = M2 + 12 + 2 * s
                gf, cv, ge = gf2[:, s % 2], cv2[:, s % 2], ge2[:, s % 2]
                if s >= 2:
                    dve.wait_ge(actT_ready, s - 1)
                for j in range(2):
                    dve.wait_ge(bank_done2, B + j + 1)
                    ft = 2 * s + j
                    a_ = PB[(B + j) % 4][:, 0:T]
                    V.tensor_scalar(gf[:, j, :], PB[(B + j) % 4][:, T:2 * T], 0.5, None, ALU.mult)
                    w = lambda i: col("conv_w", i * F2T + ft)
                    step(V.tensor_scalar(cv[:, j, :], a_, w(2), col("conv_b", ft), ALU.mult, ALU.add))
                    step(V.scalar_tensor_tensor(out=cv[:, j, 1:T], in0=a_[:, 0:T - 1], scalar=w(1), in1=cv[:, j, 1:T],
                                                op0=ALU.mult, op1=ALU.add))
                    V.scalar_tensor_tensor(out=cv[:, j, 2:T], in0=a_[:, 0:T - 2], scalar=w(0),
                                           in1=cv[:, j, 2:T], op0=ALU.mult, op1=ALU.add).then_inc(dve_evac2, 1)
                dve.wait_ge(dve_evac2, KD + 2 * s + 2)
                V.tensor_tensor(gf, gf, cv, ALU.mult).then_inc(ffn_gate, 1)
                dve.wait_ge(ffn_act, 2 * s + 1)
                step(V.tensor_scalar(ge, ge, 0.044715, 1.0, ALU.mult, ALU.add))
                V.tensor_tensor(ge, ge, cv, ALU.mult).then_inc(ffn_gate, 1)
                dve.wait_ge(ffn_act, 2 * s + 2)
                V.scalar_tensor_tensor(out=actT[:, 2 * s:2 * s + 2, :], in0=ge, scalar=1.0, in1=gf,
                                       op0=ALU.add, op1=ALU.mult).then_inc(actT_ready, 1)
            dve.wait_ge(down_slots, 6)
            for k in range(KD):
                V.tensor_tensor(xT[:, k, :], xT[:, k, :], PB[k // 2][:, (k % 2) * T:(k % 2) * T + T], ALU.add)\
                 .then_inc(x_mid, 1)
            dve.wait_ge(x_mid, 4 * KD)
            dve.wait_ge(root_ready, 8)
            step(V.reciprocal(rstd, rstd))
            for k in range(KD):
                V.scalar_tensor_tensor(out=fT[:, k, :], in0=xT[:, k, :], scalar=col("norm_final", k), in1=rstd,
                                       op0=ALU.mult, op1=ALU.mult).then_inc(final_ready, 1)

        @block.tensor
        def _(pe):
            mm = nc.tensor.matmul

            def sum_squares(sq, bank, n):
                pe.wait_ge(sq_ready, n)
                for k in range(KD):
                    ins = mm(bank[:, 0:T], ones, sq[:, k, :], start=k == 0, stop=k == KD - 1)
                ins.then_inc(sum_ready, 1)

            pe.wait_ge(consts_in, 48)
            sum_squares(sqx, AS[0], 1)
            sum_squares(sqc, AS[1], 2)
            pe.wait_ge(cs_ready, 1)
            for n in range(12):
                pe.wait_ge(landed[n % RING], 16 * (n // RING + 1))
                W = slot(n, KD, 512)
                for c in range(4):
                    for k in range(KD):
                        ins = mm(PT[:, 8 * n + 2 * c:8 * n + 2 * c + 2], W[:, k, c * P:c * P + P], cs[:, k, :],
                                 start=k == 0, stop=k == KD - 1)
                ins.then_inc(mod_slots, 1)

            B = [0]
            state = [BANKS1, bank_done, act_evac, dve_evac, landed]

            def bank():
                banks, _, act_s_, dve_s_, _ = state
                n = B[0]
                B[0] += 1
                if n >= 4:
                    who = banks[n - 4]
                    pe.wait_ge(act_s_ if who == "act" else dve_s_, evacs(banks, n - 3, who))
                return PB[n % 4]

            def need(n):
                if state[0] is BANKS1:
                    pe.wait_ge(landed[n % RING], 16 * (n // RING + 1))
                else:
                    pe.wait_ge(landed2[n % RING], land2(n))

            def features(W, src, c0, K=KD):
                pb = bank()
                for c in range(2):
                    for k in range(K):
                        ins = mm(pb[:, c * T:c * T + T], W[:, k, (c0 + c) * P:(c0 + c) * P + P], src[:, k, :],
                                 start=k == 0, stop=k == K - 1)
                ins.then_inc(state[1], 1)

            def tokens(W, src, tt, n=512):
                pb = bank()
                for k in range(KD):
                    ins = mm(pb[:, 0:n], src[:, k, tt * P:tt * P + P], W[:, k, 0:n], start=k == 0, stop=k == KD - 1)
                ins.then_inc(state[1], 1)

            pe.wait_ge(h_ready, 2 * KD)
            need(12)
            for src in (hT, hcT):
                for b in range(2):
                    features(slot(12, KD, 512), src, 2 * b)
            need(13)
            for src in (hT, hcT):
                for tt in range(TT):
                    tokens(slot(13, KD, 512), src, tt)
            need(14)
            for src in (hT, hcT):
                pb = bank()
                for tt in range(TT):
                    for k in range(KD):
                        ins = mm(pb[:, tt * 256:tt * 256 + 256], src[:, k, tt * P:tt * P + P],
                                 slot(14, KD, 256)[:, k, :], start=k == 0, stop=k == KD - 1)
                ins.then_inc(bank_done, 1)
            need(15)
            for b in range(2):
                features(slot(15, KD, 512), hT, 2 * b)
            need(16)
            for tt in range(TT):
                tokens(slot(16, KD, 512), hT, tt)

            def attention(u0, widths, scores, value, Pb, PTb, ot, gate):
                def s(u):
                    if u >= 2:
                        pe.wait_ge(exp_done, u0 + u - 1)
                    for q, k, at in scores(u):
                        ins = mm(AS[u % 2][:, at:at + k.shape[-1]], q, k, start=True, stop=True)
                    ins.then_inc(scores_ready, 1)

                def turn(u):
                    pe.wait_ge(exp_done, u0 + u + 1)
                    if u >= 1:
                        pe.wait_ge(turned_copied, u0 + u)
                    for c in range(widths[u] // P):
                        ins = nc.tensor.transpose(PT[:, c * P:c * P + P], Pb[:, u % 2, c * P:c * P + P], ident)
                    ins.then_inc(turned_ready, 1)

                def pv(u):
                    h = u % NH
                    pe.wait_ge(turned_copied, u0 + u + 1)
                    if h == 0:
                        pe.wait_ge(att_tile, u0 // 8 + u // 8)
                    n = widths[u] // P
                    for c in range(n):
                        ins = mm(AO[:, h * DH:h * DH + DH], PTb[:, u % 2, c * P:c * P + P], value(u, c),
                                 start=c == 0, stop=c == n - 1)
                    ins.then_inc(pv_done, 1)

                def out_tile(tile):
                    pe.wait_ge(att_tile, u0 // 8 + tile + 1)
                    pb = bank()
                    for c in range(4):
                        ins = nc.tensor.transpose(pb[:, c * P:c * P + P], ot[:, c * P:c * P + P], ident)
                    ins.then_inc(state[1], 1)

                s(0)
                for u in range(16):
                    if u < 15:
                        s(u + 1)
                    turn(u)
                    if u >= 1:
                        pv(u - 1)
                    if u == 10:
                        out_tile(0)
                    if gate and u in GATE_AFTER:
                        gate(GATE_AFTER[u])
                pv(15)
                out_tile(1)

            def part(ap3, h):
                return ap3[DH * (h % 2):DH * (h % 2) + DH, h // 2]

            def na_scores(u):
                h, tt = u % NH, u // NH
                q = part(qaT, h)[:, tt * P:tt * P + P]
                return [(q, part(kaT, h), 0)]

            pe.wait_ge(act_evac, B1_HEAD)
            attention(0, [512] * 16, na_scores, lambda u, c: Va[:, c, (u % 8) * DH:(u % 8) * DH + DH],
                      Pm, PTs, otok, None)
            pe.wait_ge(qb_ready, 1)
            for tt in range(TT):
                pb = bank()
                for c in range(4):
                    ins = nc.tensor.transpose(pb[:, c * P:c * P + P], qb[:, tt, c * P:c * P + P], ident)
                ins.then_inc(bank_done, 1)
            for g in range(NKV):
                pb = bank()
                for i in range(4):
                    ins = nc.tensor.transpose(pb[:, i * P:i * P + P], kdup[:, i, g * P:g * P + P], ident)
                ins.then_inc(bank_done, 1)

            def gqa_scores(u):
                h, tt = u % NH, u // NH
                q = part(qbT, h)[:, tt * P:tt * P + P]
                return [(q, kbT[DH * (h % 2):DH * (h % 2) + DH, h // 4, :], 0)]

            def gate1(b):
                n = 17 + b // 2
                if b % 2 == 0:
                    need(n)
                features(slot(n, KD, 512), hT, 2 * (b % 2))

            pe.wait_ge(act_evac, B1_HEAD + 2 + 4)
            attention(16, [512] * 16, gqa_scores, lambda u, c: kvb[:, c, 128 + DH * (u % 8 // 4):192 + DH * (u % 8 // 4)],
                      Pm, PTs, otok, gate1)

            def branches(na, nb, oa, ob, ready_sem, ready_n):
                pe.wait_ge(ready_sem, ready_n)
                need(na)
                need(nb)
                for j in range(KD):
                    pb = bank()
                    for c, (n, o) in enumerate(((na, oa), (nb, ob))):
                        for k in range(4):
                            ins = mm(pb[:, c * T:c * T + T], slot(n, 4, D)[:, k, j * P:j * P + P], o[:, k, :],
                                     start=k == 0, stop=k == 3)
                    ins.then_inc(state[1], 1)

            branches(21, 22, oaT, obT, act_evac, evacs(BANKS1, M1, "act"))
            pe.wait_ge(merged_ready, KD)
            for n in range(2):
                need(23 + n)
                for b in range(2):
                    features(slot(23 + n, KD, 512), mergedT, 2 * b)
            sum_squares(sqy, AS[0], 3)
            sum_squares(sqy, AS[0], 4)

            pe.wait_ge(router_in, 16)
            pe.wait_ge(h_ready, 3 * KD)
            pe.wait_ge(act_evac, evacs(BANKS1, len(BANKS1), "act"))
            for tt in range(TT):
                for k in range(KD):
                    ins = mm(AS[0][:, tt * NE:tt * NE + NE], hT[:, k, tt * P:tt * P + P], wr[:, k, :],
                             start=k == 0, stop=k == KD - 1)
            ins.then_inc(route_pe, 1)
            for c in range(4):
                for kk in range(4):
                    k = 4 * (c % 2) + kk
                    ins = nc.tensor.transpose(PB[c][:, kk * P:kk * P + P], hT[:, k, (c // 2) * P:(c // 2) * P + P],
                                              ident)
                ins.then_inc(h2tok_t, 1)
            pe.wait_ge(route_dve, 2)
            for tt in range(TT):
                for s in range(tt + 1):
                    mm(AS[1][:, tt * NE:tt * NE + NE], tri[:, s, tt * P:tt * P + P], sel[:, s, :],
                       start=s == 0, stop=s == tt)
            for s in range(TT):
                ins = mm(AO[0:NE, 0:1], sel[:, s, :], ones[:, 0:1], start=s == 0, stop=s == 1)
            ins.then_inc(route_pe, 1)
            pe.wait_ge(route_dve, 4)
            mm(AO[0:NE, 1:2], C("tri32")[0:NE, :], eblk[:, 2:3], start=True, stop=True).then_inc(route_pe, 1)
            for tt in range(TT):
                nc.tensor.transpose(PT[0:NE, tt * P:tt * P + P], POSI[:, tt, 0:NE], ident)
                ins = nc.tensor.transpose(PT[0:NE, T + tt * P:T + tt * P + P], WI[:, tt, 0:NE], ident)
            ins.then_inc(route_pe, 1)
            pe.wait_ge(route_dve, 6)
            for tt in range(TT):
                mm(AO[:, 8 + tt * EXTRA:8 + (tt + 1) * EXTRA], posT[:, tt * P:tt * P + P], OH[:, NE:ITEMS],
                   start=True, stop=False)
                mm(AO[:, 8 + tt * EXTRA:8 + (tt + 1) * EXTRA], ones[0:NE, :], eblk[:, 48:64], start=False, stop=True)
            for tt in range(TT):
                ins = mm(AO[:, 64 + tt * EXTRA:64 + (tt + 1) * EXTRA], wT[:, tt * P:tt * P + P], OH[:, NE:ITEMS],
                         start=True, stop=True)
            ins.then_inc(route_pe, 1)
            mm(AO[0:1, 128:128 + EXTRA], C("eid")[0:NE, :], OH[:, NE:ITEMS], start=True, stop=True)
            mm(AO[0:1, 160:161], eblk[:, 2:3], ones[0:NE, 0:1], start=True, stop=True).then_inc(route_pe, 1)
            pe.wait_ge(bgu_in, 32)
            pe.wait_ge(h2tok_c, 4)
            for k in range(KD):
                ins = mm(sum_at(k), bdn[:, k * P:k * P + P], wT[:, :], start=k % 2 == 0, stop=False,
                         skip_group_check=True)
            ins.then_inc(up_slot, RING)

            halves = [(slice(CAP * b, CAP * b + CAP), slice(512 * b, 512 * b + 512)) for b in range(2)]

            def gather():
                for tt in range(TT):
                    for parts, feats in halves:
                        ins = mm(PT[parts, :], Sel[:, tt, :], h2tok[:, tt, feats], start=tt == 0, stop=tt == TT - 1)
                ins.then_inc(gathered, 1)

            def turn(bank_, src):
                for c in range(4):
                    ins = nc.tensor.transpose(bank_[:, c * P:c * P + P], src[:, c * P:c * P + P], ident)
                return ins

            def combine():
                for k in (0, 4, 1, 5, 2, 6, 3, 7):
                    half = slice(CAP * (k // 4), CAP * (k // 4) + CAP)
                    ins = mm(sum_at(k), yb[half, (k % 4) * P:(k % 4) * P + P], SelWT[half, :],
                             start=False, stop=False, skip_group_check=True)
                return ins

            pe.wait_ge(sel_ready, 1)
            gather()
            pe.wait_ge(xg_ready, 1)
            turn(AO, xg).then_inc(xg_t, 1)
            pe.wait_ge(route_dve, 7)
            n_items = pe.value_load(table[0:1, ITEMS:ITEMS + 1], min_val=NE, max_val=ITEMS - 1)
            with pe.Fori(0, n_items) as i:
                pe.wait_ge(ohb_ready, i + 1)
                for n in range(2):
                    for parts, feats in halves:
                        ins = mm(AS[n][parts, :], OHb[:, :], bgu[:, n * D + feats.start:n * D + feats.stop],
                                 start=True, stop=False)
                ins.then_inc(bias_added, 1)
                pe.wait_ge(xe_ready, i + 1)
                for s in range(4):
                    pe.wait_ge(landed[s], i * 16 + 16 * prior[s] + 16)
                    W = slot(s, 2, 2 * D)
                    for kk in range(2):
                        k = 2 * s + kk
                        for n in range(2):
                            for parts, feats in halves:
                                ins = mm(AS[n][parts, :], xe[:, k % 4, k // 4, :],
                                         W[:, kk, n * D + feats.start:n * D + feats.stop],
                                         start=False, stop=k == KD - 1)
                    ins.then_inc(up_slot, 1)
                    if s == 2:
                        pe.wait_ge(sel_ready, i + 2)
                        pe.wait_ge(selwt_c, i + 1)
                        gather()
                pe.wait_ge(xg_ready, i + 2)
                pe.wait_ge(yb_c, i + 1)
                turn(AO, xg).then_inc(xg_t, 1)
                combine()
                pe.wait_ge(actv_ready, i + 1)
                turn(PT, act_t).then_inc(act_turned, 1)
                pe.wait_ge(act_s_ready, i + 1)
                pe.wait_ge(xe_ready, i + 2)
                for s in range(4, 6):
                    pe.wait_ge(landed[s], i * 16 + 16 * prior[s] + 16)
                    W = slot(s, 4, D)
                    for kk in range(4):
                        for parts, feats in halves:
                            ins = mm(AO[parts, :], act_s[:, kk, s - 4, :], W[:, kk, feats],
                                     start=s == 4 and kk == 0, stop=s == 5 and kk == 3)
                    ins.then_inc(up_slot, 1)
                    if s == 4:
                        pe.wait_ge(selw_ready, i + 1)
                        for tt in range(TT):
                            ins = nc.tensor.transpose(PT[:, tt * P:tt * P + P], SelW[:, tt, :], ident)
                        ins.then_inc(selwt_t, 1)
            pe.wait_ge(selwt_c, n_items + 1)
            pe.wait_ge(yb_c, n_items + 1)
            combine().then_inc(moe_done, 1)
            sum_squares(sqf, AS[0], 5)
            sum_squares(sqf, AS[0], 6)

            B[0] = 0
            state[:] = [BANKS2, bank_done2, act_evac2, dve_evac2, landed2]
            pe.wait_ge(h_ready, 4 * KD)
            pe.wait_ge(small2_in, 48)
            for k in range(KD):
                ins = mm(PT[0:16, 0:T], wlr[:, k, 0:16], hT[:, k, :], start=k == 0, stop=k == KD - 1)
            ins.then_inc(gla_pe, 1)
            for tt in range(TT):
                for k in range(KD):
                    ins = mm(AS[1][:, tt * NH:(tt + 1) * NH], hT[:, k, tt * P:tt * P + P], wlr[:, k, 16:24],
                             start=k == 0, stop=k == KD - 1)
            ins.then_inc(gla_pe, 1)
            pe.wait_ge(gla_act, 1)
            for j in range(2):
                ins = mm(AO[:, j * T:j * T + T], aw2[:, j * P:j * P + P], glrT, start=True, stop=True)
            ins.then_inc(gla_pe, 1)
            need(0)
            for b in range(2):
                features(slot(0, KD, 512), hT, 2 * b)
            for n in range(1, 6):
                need(n)
                for tt in range(TT):
                    tokens(slot(n, KD, 512), hT, tt)
            pe.wait_ge(gla_dve, 3)
            for h in range(4):
                for n in range(NCH):
                    q = part(qe, h)[:, n * CHUNK:(n + 1) * CHUNK]
                    k_ = part(ke, h)[:, n * CHUNK:(n + 1) * CHUNK]
                    m0 = CHUNK * (n % 2)
                    at = ((n // 2) * 2 + h // 2) * CHUNK
                    ins = mm(AS[h % 2][m0:m0 + CHUNK, at:at + CHUNK], k_, q, start=True, stop=True)
            ins.then_inc(gla_pe, 1)
            for tt in range(TT):
                for j in range(2):
                    ins = nc.tensor.transpose(PT[:, tt * 256 + j * P:tt * 256 + (j + 1) * P],
                                              kd[:, j, tt * P:tt * P + P], ident)
            ins.then_inc(gla_pe, 1)
            pe.wait_ge(gla_act, 9)
            pe.wait_ge(act_evac2, 4)
            for n in range(3):
                m0 = CHUNK * (n % 2)
                for h in range(4):
                    d0 = DH * (h % 2)
                    at = kv_at[n] + (h // 2) * P
                    ins = mm(kv_bank[n][d0:d0 + DH, at:at + P], kdtok[m0:m0 + CHUNK, n // 2, h * DH:h * DH + DH],
                             gv[m0:m0 + CHUNK, n // 2, h * P:h * P + P], start=True, stop=True)
                if n:
                    ins.then_inc(gla_pe, 1)
            pe.wait_ge(gla_dve, 5)
            for n in range(NCH):
                m0 = CHUNK * (n % 2)
                for h in range(4):
                    ins = mm(AS[n // 2][m0:m0 + CHUNK, h * P:h * P + P],
                             AT[m0:m0 + CHUNK, n // 2, h * CHUNK:(h + 1) * CHUNK],
                             gv[m0:m0 + CHUNK, n // 2, h * P:h * P + P], start=True, stop=True)
                    if n:
                        at = (n // 2) * 256 + (h // 2) * P
                        ins = mm([AO, PT][h % 2][m0:m0 + CHUNK, at:at + P], part(qe, h)[:, n * CHUNK:(n + 1) * CHUNK],
                                 St[DH * (h % 2):DH * (h % 2) + DH, n - 1, h // 2, :], start=True, stop=True)
            ins.then_inc(gla_pe, 1)
            pe.wait_ge(gla_act, 10)
            logf = Z[:, 512:528].rearrange("p (t h) -> p t h", h=NH)
            for tt in range(TT):
                for s in range(tt + 1):
                    ins = mm(PT[:, tt * NH:(tt + 1) * NH], tri[:, s, tt * P:tt * P + P], logf[:, s, :],
                             start=s == 0, stop=s == tt)
            ins.then_inc(gla_pe, 1)
            for pair in range(4):
                if pair == 1:
                    pe.wait_ge(gla_dve, 6)
                if pair == 2:
                    pe.wait_ge(cb_ready, 1)
                for hh in range(2):
                    for s in range(TT):
                        lf = logf[:, s, 2 * pair + hh:2 * pair + hh + 1].to_broadcast([P, P])
                        ins = mm(c_banks[pair][:, hh * T:hh * T + T], lf, tri[:, s, :], start=s == 0, stop=s == 1)
                ins.then_inc(gla_pe, 1)
            pe.wait_ge(gla_dve, 8)
            for tt in range(TT):
                pb = bank()
                for c in range(4):
                    ins = nc.tensor.transpose(pb[:, c * P:c * P + P], og[:, tt, c * P:c * P + P], ident)
                ins.then_inc(bank_done2, 1)
            pe.wait_ge(qb_ready, 2)
            for tt in range(TT):
                for src in (fq, fk):
                    pb = bank()
                    for c in range(4):
                        ins = nc.tensor.transpose(pb[:, c * P:c * P + P], src[:, tt, c * P:c * P + P], ident)
                    ins.then_inc(bank_done2, 1)

            def fox_scores(u):
                h, tt = u % NH, u // NH
                return [(part(fqT, h)[:, tt * P:tt * P + P], part(fkT, h)[:, 0:P * (tt + 1)], 0)]

            def gate2(b):
                n = 6 + b // 2
                if b % 2 == 0:
                    need(n)
                features(slot(n, KD, 512), hT, 2 * (b % 2))

            pe.wait_ge(act_evac2, G2)
            pe.wait_ge(cb_ready, 4)
            attention(32, [P] * 8 + [T] * 8, fox_scores, lambda u, c: fv[:, c, (u % 8) * DH:(u % 8) * DH + DH],
                      Pm2, PT2, otok2, gate2)
            branches(10, 11, ogT, ofT, act_evac2, evacs(BANKS2, M2, "act"))
            pe.wait_ge(merged_ready2, KD)
            for n in range(2):
                need(12 + n)
                for b in range(2):
                    features(slot(12 + n, KD, 512), merged2, 2 * b)
            sum_squares(sq2, AS[0], 7)
            pe.wait_ge(h_ready, 5 * KD)
            for n in range(11):
                need(UP0 + n)
                W = slot(UP0 + n, KD, 512)
                for j in range(2):
                    pb = bank()
                    for c in range(2):
                        for k in range(KD):
                            ins = mm(pb[:, c * T:c * T + T], W[:, k, c * 256 + j * P:c * 256 + j * P + P],
                                     hT[:, k, :], start=k == 0, stop=k == KD - 1)
                    ins.then_inc(bank_done2, 1)
            pe.wait_ge(dve_evac2, KD + 22)
            for n in range(6):
                need(DN0 + n)
                pe.wait_ge(actT_ready, min(2 * n + 2, 11))
                K = stream2[DN0 + n].shape[1]
                W = slot(DN0 + n, K, D)
                for j in range(KD):
                    for k in range(K):
                        ins = mm(PB[j // 2][:, (j % 2) * T:(j % 2) * T + T], W[:, k, j * P:j * P + P],
                                 actT[:, 4 * n + k, :], start=n == 0 and k == 0 and j % 2 == 0, stop=n == 5 and k == K - 1,
                                 skip_group_check=True)
                ins.then_inc(down_slots, 1)
            sum_squares(sq2, AS[0], 8)


INPUTS = ["w_mod", "w_in", "w_out_a", "w_out_b", "w_o", "w_router", "b_gu", "b_dn", "w_gu", "w_dn"]
RENAMED = {"w_in_2": "w_in_2", "alpha_w2": "gla_alpha_w2_2", "w_gla": "w_gla_branch_2", "w_fox": "w_fox_branch_2",
           "w_out_2": "w_out_2", "w_up": "w_up_2", "w_down": "w_down_2"}


def kernel(**inputs):
    from concourse.bass_utils import run_bass_kernel_spmd as run
    import concourse.bacc as bacc

    get = lambda name: np.asarray(inputs[name])

    def features_first(a):
        return np.ascontiguousarray(a.T.reshape(KD, P, -1).transpose(1, 0, 2))

    def columns(a):
        return a.reshape(-1, P).T

    arrays = {name: np.ascontiguousarray(get(name)[0]) for name in INPUTS}
    arrays |= {name: np.ascontiguousarray(get(theirs)[0]) for name, theirs in RENAMED.items()}
    arrays["xT"] = features_first(get("x")[0])
    arrays["ctxT"] = features_first(get("ctx")[0])
    arrays["cst"] = constants()
    both = np.stack([get("c")[0], get("c_ctx")])
    parts = [columns(get(n)[0]) for n in ("b_mod", "g_pre_mix", "g_post_mix", "g_pre_ffn", "g_post_ffn",
                                          "norm_mix_g_2", "gla_alpha_b_2", "gate_b_2", "norm_ffn_g_2", "conv_w_2",
                                          "conv_b_2")]
    parts += [columns(get("norm_final_g_2")), features_first(both).reshape(P, 2 * KD)]
    arrays["cols"] = np.ascontiguousarray(np.concatenate(parts, axis=1))
    arrays["rows"] = np.concatenate([get(n)[0].reshape(-1) for n in (
        "g_qnorm", "g_knorm", "fox_q_norm_g_2", "fox_k_norm_g_2", "gla_out_norm_g_2", "fox_forget_b_2", "b_router")])
    padded = np.pad(get("rpb")[0].reshape(NH * 15, 31), ((0, 0), (48, 48)))
    arrays["rpb"] = np.ascontiguousarray(np.broadcast_to(padded[:, None, :], (NH * 15, GRID_W, 127)))

    nc = bacc.Bacc("TRN2", target_bir_lowering=False, num_devices=1)
    A = {n: nc.dram_tensor(n + "_dram", a.shape, mybir.dt.from_np(a.dtype), kind="ExternalInput").ap()
         for n, a in arrays.items()}
    out = nc.dram_tensor("out_dram", (P, KD, T), F32, kind="ExternalOutput").ap()
    two_blocks(nc, A, out)
    r = run(nc, [{n + "_dram": a for n, a in arrays.items()}], core_ids=[0])
    got = r.results[0]["out_dram"]
    return np.ascontiguousarray(got.transpose(2, 1, 0)).reshape(1, T, D)
```

```python
from contextlib import ExitStack

import concourse.bass as bass
import numpy as np
from concourse import mybir

F32 = mybir.dt.float32
I32 = mybir.dt.int32
ALU = mybir.AluOpType
ACT = mybir.ActivationFunctionType
AX = mybir.AxisListType

P = 128
D = 1024
KD = D // P
T = 256
TT = T // P
GRID_W = 64
ROWS = T // GRID_W
DH = 64
NH = 8
NKV = 2
WIN_R, WIN_C = 8, 16
NE = 32
TOPK = 4
CAP = 64
EXTRA = 16
ITEMS = NE + EXTRA
FF2 = 2816
F2T = FF2 // P
RING = 6
SLOT = 4096
EPS = 1e-6
NEG = -1.0e30
SENTINEL = -3.0e38
FAR = 4096.0
CHUNK = 64
NCH = T // CHUNK
TAU = 16.0


def layout(sizes):
    at, out = 0, {}
    for name, n in sizes:
        out[name] = (at, at + n)
        at += n
    return out, at


CONST, CONST_N = layout([
    ("ident", P), ("ones", P), ("tri", TT * T), ("causal", P), ("gla_mask", CHUNK), ("window", GRID_W),
    ("iota", P), ("cos", TT * DH), ("sin", TT * DH), ("carry", T), ("tri32", NE), ("eid", 1), ("eps", 1),
    ("one", 1),
])
COLS, COLS_N = layout([
    ("b_mod", 48), ("g_pre_mix", KD), ("g_post_mix", KD), ("g_pre_ffn", KD), ("g_post_ffn", KD),
    ("norm_mix", KD), ("alpha_b", 2), ("gate_b", 2 * KD), ("norm_ffn", KD), ("conv_w", 3 * F2T),
    ("conv_b", F2T), ("norm_final", KD), ("c", 2 * KD),
])
ROWS_L, ROWS_N = layout([
    ("g_q", DH), ("g_k", DH), ("fox_q", DH), ("fox_k", DH), ("gla_out", 512), ("forget_b", NH), ("b_router", NE),
])


def constants():
    c = np.zeros((P, CONST_N), np.float32)

    def put(name, a):
        lo, hi = CONST[name]
        c[: a.shape[0], lo:hi] = a.reshape(a.shape[0], -1)

    p = np.arange(P)
    t = np.arange(T)
    put("ident", np.eye(P))
    put("ones", np.ones((P, P)))
    s = (np.arange(TT)[None, :] * P + p[:, None])
    put("tri", (s[:, :, None] <= t[None, None, :]).astype(np.float32))
    put("causal", np.where(p[None, :] <= p[:, None], 0.0, NEG))
    put("gla_mask", (p[:, None] % CHUNK <= np.arange(CHUNK)[None, :]).astype(np.float32))
    w = p % GRID_W
    c0 = np.clip(w - WIN_C // 2, 0, GRID_W - WIN_C)
    k = np.arange(GRID_W)
    put("window", np.where((k[None, :] >= c0[:, None]) & (k[None, :] < c0[:, None] + WIN_C), 0.0, NEG))
    put("iota", np.broadcast_to((p % CAP).astype(np.float32), (P, P)))
    nf = DH // 4
    freqs = (np.float32(10000.0) ** (-np.arange(nf, dtype=np.float32) / nf)).astype(np.float32)
    cos, sin = np.zeros((P, TT, DH)), np.zeros((P, TT, DH))
    for blk, pos in enumerate((s // GRID_W, s % GRID_W)):
        ang = pos.astype(np.float32)[:, :, None] * freqs
        at = blk * 2 * nf
        cos[:, :, at:at + nf] = cos[:, :, at + nf:at + 2 * nf] = np.cos(ang)
        sin[:, :, at:at + nf], sin[:, :, at + nf:at + 2 * nf] = -np.sin(ang), np.sin(ang)
    put("cos", cos)
    put("sin", sin)
    put("carry", np.broadcast_to((t % CHUNK != 0).astype(np.float32), (P, T)))
    e = np.arange(NE)
    put("tri32", (e[:, None] <= e[None, :]).astype(np.float32))
    put("eid", e[:, None].astype(np.float32))
    put("eps", np.full((P, 1), EPS))
    put("one", np.ones((P, 1)))
    return c


W_IN_SLOTS = [(1024, 1280), (1792, 2304), (0, 512), (512, 1024), (1280, 1792)] + \
             [(2304 + 512 * i, 2816 + 512 * i) for i in range(4)]
LR0 = 1536
FQ0 = LR0 + 16
FF0 = FQ0 + 3 * 512
G20 = FF0 + NH
W_IN2_SLOTS = [(0, 512), (512, 1024), (1024, 1536), (FQ0, FQ0 + 512), (FQ0 + 512, FQ0 + 1024),
               (FQ0 + 1024, FQ0 + 1536)] + [(G20 + 512 * i, G20 + 512 * (i + 1)) for i in range(4)]

GATE_AFTER = {u: u // 2 for u in range(1, 16, 2)}
HEAD1 = 2 + 2 + 2 + 4 + 4 + 4 + 2
G1 = HEAD1 + 2 + 2
BANKS1 = ["act", "dve"] + ["act"] * (HEAD1 - 2) + ["act", "dve"] + ["act", "dve"] + \
         ["act"] * 8 + ["dve"] * (8 + 4)
BANKS2 = ["act"] * (12 + 2 + 4 + 8) + ["dve"] * (8 + 4 + 22)


def two_blocks(nc, A, out):
    with ExitStack() as ctx:
        def sb(name, shape, dt=F32):
            return ctx.enter_context(nc.sbuf_tensor(name, shape, dt))

        def sem(name):
            return ctx.enter_context(nc.semaphore(name))

        ring = sb("ring", [P, RING, SLOT])
        xT = sb("xT", [P, KD, T])
        cst = sb("cst", [P, CONST_N])
        cols = sb("cols", [P, COLS_N])
        rows = sb("rows", [P, ROWS_N])
        ARENA = 19456
        arena = sb("arena", [P, ARENA])
        small = sb("small", [P, 1280])
        wr = sb("w_router", [P, KD, NE])
        table = sb("table", [1, ITEMS + 2], I32)
        PB = [ctx.enter_context(nc.psum_tensor(f"proj{i}", [P, 512], F32)) for i in range(4)]
        AS = [ctx.enter_context(nc.psum_tensor(f"scores{i}", [P, 512], F32)) for i in range(2)]
        PT = ctx.enter_context(nc.psum_tensor("turned", [P, 512], F32))
        AO = ctx.enter_context(nc.psum_tensor("att_out", [P, 512], F32))

        def region(at, *dims, parts=P):
            n = int(np.prod(dims))
            assert at + n <= ARENA
            v = arena[0:parts, at:at + n]
            if len(dims) == 2:
                v = v.rearrange("p (a b) -> p a b", b=dims[1])
            elif len(dims) == 3:
                v = v.rearrange("p (a b c) -> p a b c", b=dims[1], c=dims[2])
            return v

        def C(name):
            lo, hi = CONST[name]
            return cst[:, lo:hi]

        def col(name, i=0, n=1):
            lo, _ = COLS[name]
            return cols[:, lo + i:lo + i + n]

        def row(name):
            lo, hi = ROWS_L[name]
            return rows[:, lo:hi]

        small_at = [0]

        def tiny(n):
            small_at[0] += n
            assert small_at[0] <= 1280
            return small[:, small_at[0] - n:small_at[0]]

        ident, ones = C("ident"), C("ones")
        tri = C("tri").rearrange("p (a t) -> p a t", t=T)

        hT = region(0, KD, T)
        hcT = region(2048, KD, T)
        Pm = region(2048, 2, 512)
        PTs = region(3072, 2, 512)
        bias = region(4096, TT, NH, T)
        gates = region(4096, 2 * KD, T)
        sqx = region(8192, KD, T)
        qaT = region(8192, NH, T)
        kaT = [region(10240, 2, 2 * T), region(18432, 2, 2 * T)]
        Va = region(11264, 4, 512)
        ctxT = region(11264, KD, T)
        sqc = region(13312, KD, T)
        qb = region(13312, TT, 512)
        kvb = region(14336, 4, 256)
        oaT = region(15872, 4, T)
        qbT = region(13312, TT, 4, P)
        kbT = region(17408, NKV, 2 * T)
        tmp1 = region(4096, TT, 512)
        tmp2 = region(5120, TT, 512)
        rk1 = region(6144, TT, 128)
        rk2 = region(6400, TT, 128)
        kdup = region(6656, 4, 256)
        obT = region(12288, 4, T)
        mergedT = region(8192, KD, T)
        yT = region(13312, KD, T)
        sqy = region(2048, KD, T)
        h2tok = region(2048, TT, D)
        bgu = region(4096, 2048)
        bdn = region(6144, D, parts=NE)
        act_t = region(7168, 512)
        OHb = region(7680, CAP)
        logit = region(8192, TT, 40)
        lpart = region(10240, T)
        mark = region(8288, TT, 40)
        top8 = region(8384, TT, 8)
        sel = region(8416, TT, NE)
        prob = region(8480, TT, NE)
        posT = region(8544, T, parts=NE)
        wT = region(8800, T, parts=NE)
        OH = region(9056, ITEMS + 1, parts=NE)
        eblk = region(9106, 96, parts=NE)
        POSI = region(9472, TT, ITEMS + 1)
        WI = region(9600, TT, ITEMS + 1)
        Sel = region(9728, TT, CAP)
        SelW = region(11776 + 512, TT, 2 * CAP)
        SelWT = region(9984, T)
        xe = region(10240, 4, 2, CAP)
        glu = region(10752, 512)
        lin = region(11264, 512)
        esig = region(11776, 512)
        act_s = region(12544, 4, 2, CAP)
        xg = region(13056, 512)
        yb = region(13568, 512)
        sqf = region(14336, KD, T)
        fT = region(10240, KD, T)
        modrow = region(16896, 512)
        gqk = region(2048, 4, T)
        gv = region(3072, TT, 512)
        gr = region(4096, TT, 512)
        fq = region(5120, TT, 512)
        fk = region(6144, TT, 512)
        fv = region(7168, TT, 512)
        wlr = region(17408, KD, 32)
        aw2 = region(17664, 256)
        glrT = region(17920, T)
        Z = region(8896, 528)
        Z1 = region(9424, 528)
        bcum = region(9952, 2, T)
        eb = region(10464, 2, T)
        enb = region(10976, 2, T)
        kd = region(11488, 2, T)
        qe = region(12000, 2, T)
        ke = region(12512, 2, T)
        kdtok = region(13024, TT, 256)
        AT = region(13536, TT, 4 * CHUNK)
        St = region(14048, 3, 2, P)
        og = region(14816, TT, 512)
        esr = region(15840, TT, 512)
        fsq = region(10976, TT, 512)
        osq = region(9952, TT, 512)
        ogT = region(2048, 4, T)
        ofT = region(13024, 4, T)
        fqT = region(14816, 4, T)
        fkT = region(15840, 4, T)
        Cb = [region(9952, NH, P), region(10976, NH, T)]
        Pm2 = region(3072, 2, 512)
        PT2 = region(4096, 2, 512)
        gate_spans = [(5120, 8), (8192, 6), (14048, 2)]
        gate_at = [lo + 256 * j for lo, n in gate_spans for j in range(n)]
        gate2_tile = [region(lo, T) for lo in gate_at]
        merged2 = region(3072, KD, T)
        sq2 = region(12000, KD, T)
        actT = region(2048, F2T, T)
        gf2 = region(7680, 2, 2, T)
        cv2 = region(8704, 2, 2, T)
        ge2 = region(9728, 2, 2, T)

        rstd = tiny(T)
        rstd_c = tiny(T)
        cs = tiny(32 * KD).rearrange("p (k c) -> p k c", c=32)
        cse = tiny(2 * KD).rearrange("p (k c) -> p k c", c=2)
        mod = tiny(96).rearrange("p (k c) -> p k c", c=2)
        A1 = tiny(2 * KD).rearrange("p (k c) -> p k c", c=2)
        A2 = tiny(KD)
        gt1 = tiny(KD)
        gt2 = tiny(KD)
        ssq = tiny(32)
        nmax = tiny(2)
        den = tiny(2 * NH).rearrange("p (t h) -> p t h", h=NH)
        dinv = tiny(NH)
        lsum = tiny(TT)
        linv = tiny(TT)
        nm1 = tiny(TT)
        cq = tiny(TT * NH).rearrange("p (t h) -> p t h", h=NH)
        half_gate_b = tiny(2 * KD)

        landed = [sem(f"slot_landed{i}") for i in range(RING)]
        consts_in = sem("consts_in")
        x_in = sem("x_in")
        ctx_in = sem("ctx_in")
        bias_in = sem("bias_in")
        bias_masked = sem("bias_masked")
        qa_zeroed = sem("qa_zeroed")
        router_in = sem("router_in")
        bgu_in = sem("bgu_in")
        bgu_zeroed = sem("bgu_zeroed")
        small2_in = sem("small2_in")
        small2_zeroed = sem("small2_zeroed")
        out_done = sem("out_done")
        act_step = sem("act_step")
        dve_step = sem("dve_step")
        bank_done = sem("bank_done")
        act_evac = sem("act_evac")
        dve_evac = sem("dve_evac")
        cs_ready = sem("cs_ready")
        mod_slots = sem("mod_slots_used")
        cs_exp = sem("cs_exp")
        mod_ready = sem("mod_ready")
        sq_ready = sem("squares_ready")
        sum_ready = sem("sum_of_squares_ready")
        root_ready = sem("root_ready")
        scaled_ready = sem("scaled_ready")
        h_ready = sem("h_ready")
        hc_ready = sem("context_h_ready")
        scores_ready = sem("scores_ready")
        max_ready = sem("max_ready")
        exp_done = sem("exp_done")
        turned_ready = sem("turned_ready")
        turned_copied = sem("turned_copied")
        pv_done = sem("pv_done")
        probs_ready = sem("probs_normalised")
        att_tile = sem("att_tile_copied")
        qk_sq = sem("head_squares_ready")
        qk_root = sem("head_root_ready")
        qb_ready = sem("qb_ready")
        merged_ready = sem("merged_ready")
        merged_ready2 = sem("merged_ready_b")
        x_mid = sem("x_mid_ready")
        h2tok_t = sem("h2tok_turned")
        h2tok_c = sem("h2tok_copied")
        route_pe = sem("route_pe")
        route_dve = sem("route_dve")
        route_act = sem("route_act")
        logits_copied = sem("logits_copied")
        logits_turned = sem("logits_turned")
        sel_ready = sem("sel_ready")
        gathered = sem("gathered")
        xg_ready = sem("gathered_copied")
        xg_t = sem("gathered_turned")
        xe_ready = sem("xe_ready")
        ohb_ready = sem("expert_onehot_ready")
        bias_added = sem("up_biases_added")
        up_slot = sem("expert_slot_used")
        glu_ready = sem("glu_ready")
        esig_ready = sem("esig_ready")
        actv_ready = sem("activation_ready")
        act_turned = sem("activation_turned")
        act_s_ready = sem("activation_copied")
        selw_ready = sem("selw_ready")
        selwt_t = sem("selw_turned")
        selwt_c = sem("selw_copied")
        yb_c = sem("yb_copied")
        moe_dve = sem("moe_dve_step")
        moe_done = sem("moe_done")
        landed2 = [sem(f"slot_landed_b{i}") for i in range(RING)]
        bank_done2 = sem("bank_done_b")
        act_evac2 = sem("act_evac_b")
        dve_evac2 = sem("dve_evac_b")
        gla_pe = sem("gla_pe")
        gla_dve = sem("gla_dve")
        gla_act = sem("gla_act")
        cb_ready = sem("cb_ready")
        down_slots = sem("down_slots_used")
        ffn_act = sem("ffn_act")
        ffn_gate = sem("ffn_gate")
        actT_ready = sem("actT_ready")
        final_ready = sem("final_ready")

        def w_cols(w, lo, hi):
            return w.rearrange("(k p) n -> p k n", p=P)[:, :, lo:hi]

        mod_cols = [w_cols(A["w_mod"], 2048 * g, 2048 * g + 2048)[:, 2 * n:2 * n + 2, :]
                    for g in range(3) for n in range(4)]
        in_cols = [w_cols(A["w_in"], lo, hi) for lo, hi in W_IN_SLOTS]
        stream1 = mod_cols[:4] + in_cols[:5] + mod_cols[4:] + in_cols[5:]
        stream1 += [w_cols(A["w_out_a"], 0, D), w_cols(A["w_out_b"], 0, D)]
        stream1 += [w_cols(A["w_o"], 512 * n, 512 * n + 512) for n in range(2)]
        N1 = len(stream1)
        used1 = [(mod_slots, n + 1) for n in range(4)]
        used1 += [(bank_done, 2 + v) for v in (2, 4, 8, 16, 18)]
        used1 += [(mod_slots, n + 1) for n in range(4, 12)]
        at = G1
        gate_bank_no = []
        for u in range(16):
            if u in GATE_AFTER:
                at += 1
                gate_bank_no.append(at)
        used1 += [(bank_done, gate_bank_no[2 * s + 1]) for s in range(4)]
        M1 = G1 + 8
        used1 += [(bank_done, M1 + 8)] * 2
        used1 += [(bank_done, M1 + 8 + 2), (bank_done, M1 + 8 + 4)]
        assert len(used1) == N1 and M1 + 12 == len(BANKS1)
        prior = [len([n for n in range(N1) if n % RING == s]) for s in range(RING)]
        last1 = [max(n for n in range(N1) if n % RING == s) for s in range(RING)]

        stream2 = [w_cols(A["w_in_2"], lo, hi) for lo, hi in W_IN2_SLOTS]
        stream2 += [w_cols(A["w_gla"], 0, D), w_cols(A["w_fox"], 0, D)]
        stream2 += [w_cols(A["w_out_2"], 512 * n, 512 * n + 512) for n in range(2)]
        UP0 = len(stream2)
        stream2 += [None] * 11
        DN0 = len(stream2)
        stream2 += [A["w_down"][512 * n:min(512 * n + 512, FF2), :].rearrange("(k p) n -> p k n", p=P)
                    for n in range(6)]
        N2 = len(stream2)
        used2 = [(bank_done2, 2 * n + 2) for n in range(6)]
        at = 12 + 2 + 4
        gate_bank_no2 = []
        for u in range(16):
            if u in GATE_AFTER:
                at += 1
                gate_bank_no2.append(at)
        used2 += [(bank_done2, gate_bank_no2[2 * s + 1]) for s in range(4)]
        M2 = 12 + 2 + 4 + 8
        used2 += [(bank_done2, M2 + 8)] * 2 + [(bank_done2, M2 + 10), (bank_done2, M2 + 12)]
        used2 += [(bank_done2, M2 + 12 + 2 * n + 2) for n in range(11)]
        used2 += [(down_slots, n + 1) for n in range(6)]
        assert len(used2) == N2 and M2 + 12 + 22 == len(BANKS2)

        G2 = 12 + 2 + 4

        def slot(n, *dims):
            v = ring[:, n % RING, 0:int(np.prod(dims))]
            return v.rearrange("p (k c) -> p k c", c=dims[1])

        def sum_at(k):
            return PB[k // 2][:, (k % 2) * T:(k % 2) * T + T]

        kv_bank, kv_at = [AO, PT, AO], [0, 0, 256]
        c_banks = [AO, AS[0], AO, AS[1]]

        def gates_after(gate):
            return {u: (lambda b=b: gate(b)) for u, b in GATE_AFTER.items()}

        def evacs(banks, upto, who):
            return sum(b == who for b in banks[:upto])

        block = ctx.enter_context(nc.Block())

        @block.sync
        def _(sp):
            def load(n):
                src = stream1[n]
                if n >= RING:
                    sp.wait_ge(*used1[n - RING])
                sp.dma_start(slot(n, src.shape[1], src.shape[2]), src).then_inc(landed[n % RING], 16)

            sp.dma_start(xT[:], A["xT"]).then_inc(x_in, 16)
            sp.dma_start(ctxT, A["ctxT"]).then_inc(ctx_in, 16)
            for n in range(N1):
                load(n)

            def expert(e, s):
                w, n, K, N = (A["w_gu"], s, 2, 2 * D) if s < 4 else (A["w_dn"], s - 4, 4, D)
                src = w[e].rearrange("a (k p) n -> p (a k) n", p=P)[:, K * n:K * n + K, :]
                sp.dma_start(slot(s, K, N), src).then_inc(landed[s], 16)

            for s in range(RING):
                sp.wait_ge(*used1[last1[s]])
                expert(slice(0, 1), s)
            sp.wait_ge(route_dve, 7)
            n_items = sp.value_load(table[0:1, ITEMS:ITEMS + 1], min_val=NE, max_val=ITEMS - 1)
            with sp.Fori(1, n_items) as i:
                e = sp.value_load(table[0:1, bass.ds(i, 1)], min_val=0, max_val=NE - 1)
                for s in range(RING):
                    sp.wait_ge(up_slot, i * RING + (s + 1))
                    expert(bass.ds(e, 1), s)
            for n in range(N2):
                src = stream2[n]
                if n < RING:
                    sp.wait_ge(up_slot, n_items * RING + (n + 1))
                else:
                    sp.wait_ge(*used2[n - RING])
                if UP0 <= n < DN0:
                    for half in range(2):
                        c0 = half * FF2 + 256 * (n - UP0)
                        sp.dma_start(slot(n, KD, 512)[:, :, 256 * half:256 * half + 256],
                                     w_cols(A["w_up"], c0, c0 + 256)).then_inc(landed2[n % RING], 16)
                else:
                    sp.dma_start(slot(n, src.shape[1], src.shape[2]), src).then_inc(landed2[n % RING], 16)
            for c in range(2):
                sp.wait_ge(final_ready, KD // 2 * (c + 1))
                sp.dma_start(out[:, 4 * c:4 * c + 4, :], fT[:, 4 * c:4 * c + 4, :]).then_inc(out_done, 16)
            sp.wait_ge(out_done, 32)

        def land2(n):
            return 16 * sum((2 if UP0 <= m < DN0 else 1) for m in range(n + 1) if m % RING == n % RING)

        @block.gpsimd
        def _(pool):
            pool.wait_ge(h_ready, KD)
            nc.gpsimd.memset(qaT, 0.0).then_inc(qa_zeroed, 1)
            pool.wait_ge(bias_in, 16 * ROWS * ROWS)
            pool.wait_ge(consts_in, 48)
            b = bias.rearrange("p t h (r w) -> p (t h r) w", w=GRID_W)
            nc.gpsimd.tensor_tensor(b, b, C("window").unsqueeze(1).to_broadcast([P, TT * NH * ROWS, GRID_W]),
                                    ALU.add).then_inc(bias_masked, 1)
            pool.wait_ge(bgu_zeroed, 1)
            nc.gpsimd.memset(arena[:, 17408:17920], 0.0).then_inc(small2_zeroed, 1)

        @block.scalar
        def _(act):
            n_step = [0]

            def step(ins):
                n_step[0] += 1
                ins.then_inc(act_step, 1)
                act.wait_ge(act_step, n_step[0])

            act.dma_start(cst[:], A["cst"]).then_inc(consts_in, 16)
            act.dma_start(cols[:], A["cols"]).then_inc(consts_in, 16)
            act.dma_start(rows[:], A["rows"].partition_broadcast(P)).then_inc(consts_in, 16)
            act.dma_start(wr[:], A["w_router"].rearrange("(k p) n -> p k n", p=P)).then_inc(router_in, 16)

            act.wait_ge(consts_in, 48)
            cc = col("c", 0, 2 * KD).rearrange("p (k c) -> p k c", c=2)
            nc.scalar.activation(cse, cc, ACT.Tanh, scale=0.5).then_inc(cs_exp, 1)

            def squares(src, dst):
                nc.scalar.activation(dst, src, ACT.Square).then_inc(sq_ready, 1)

            def root(n, bank, dst):
                act.wait_ge(sum_ready, n)
                nc.scalar.activation(dst, bank[:, 0:T], ACT.Sqrt, scale=1.0 / D, bias=C("eps"))\
                  .then_inc(root_ready, 1)

            act.wait_ge(x_in, 16)
            squares(xT[:], sqx)
            act.wait_ge(ctx_in, 16)
            squares(ctxT, sqc)
            root(1, AS[0], rstd)
            root(2, AS[1], rstd_c)

            bank = [0]

            def evac(done, freed, dst, cols_=512, func=ACT.Copy, scale=1.0, view=None, parts=P):
                B = bank[0]
                bank[0] += 1
                act.wait_ge(done, B + 1)
                src = PB[B % 4][0:parts, 0:cols_]
                if view is not None:
                    src = src.rearrange("p (a b) -> p a b", b=view)
                nc.scalar.activation(dst, src, func, scale=scale).then_inc(freed, 1)

            ev1 = lambda dst, *a, **k: evac(bank_done, act_evac, dst, *a, **k)

            def mod_rows(g):
                B = bank[0]
                bank[0] += 2
                act.wait_ge(mod_slots, 4 * g + 4)
                nc.scalar.activation(modrow, PB[B % 4][:, :], ACT.Copy).then_inc(act_evac, 1)

            mod_rows(0)
            act.wait_ge(mod_ready, 1)
            act.wait_ge(scaled_ready, 1)
            for k in range(KD):
                nc.scalar.activation(hT[:, k, :], sqx[:, k, :], ACT.Identity, scale=A1[:, k, 0:1],
                                     bias=mod[:, k, 0:1]).then_inc(h_ready, 1)

            act.wait_ge(hc_ready, KD)
            for i in range(2):
                ev1(kvb[:, 2 * i:2 * i + 2, :], view=256)
            for i in range(2):
                ev1(qb[:, i, :])
            act.wait_ge(qk_sq, 1)
            nc.scalar.activation(ssq[:, 0:24], ssq[:, 0:24], ACT.Sqrt, scale=1.0 / DH, bias=C("eps"))\
              .then_inc(qk_root, 1)
            for src in range(2):
                for b in range(2):
                    ev1(kaT[b][:, :, src * T:src * T + T], view=T)
            for tt in range(TT):
                ev1(qbT[:, tt], view=P, scale=DH ** -0.5)
            for g in range(NKV):
                ev1(kbT[:, g, :])
            for r in range(ROWS):
                half, tt = r % 2, r // 2
                row_at = GRID_W * (2 * GRID_W - 1)
                for r2 in range(ROWS):
                    src = bass.AP(A["rpb"].tensor, A["rpb"].offset + (WIN_R - 1 - r + r2) * row_at + GRID_W - 1,
                                  [[2 * GRID_W - 2, GRID_W], [15 * row_at, NH], [1, GRID_W]])
                    dst = bias[GRID_W * half:GRID_W * half + GRID_W, tt, :, GRID_W * r2:GRID_W * (r2 + 1)]
                    act.dma_start(dst, src).then_inc(bias_in, 16)
            for i in range(4):
                ev1(Va[:, i, :])
            act.wait_ge(qa_zeroed, 1)
            for b in range(2):
                B = bank[0]
                bank[0] += 1
                act.wait_ge(bank_done, B + 1)
                for odd in range(2):
                    half = slice(DH * odd, DH * odd + DH)
                    ins = nc.scalar.activation(
                        qaT[half, 4 * b:4 * b + 4, :].rearrange("p (a o) t -> p a o t", o=2)[:, :, odd, :],
                        PB[B % 4][half, :].rearrange("p (a t) -> p a t", t=T), ACT.Copy, scale=DH ** -0.5)
                ins.then_inc(act_evac, 1)

            def attention(u0, widths, Pb, PTb, oT, after):
                def copy(u):
                    act.wait_ge(turned_ready, u0 + u + 1)
                    if u >= 2:
                        act.wait_ge(pv_done, u0 + u - 1)
                    nc.scalar.activation(PTb[:, u % 2, 0:widths[u]], PT[:, 0:widths[u]], ACT.Copy)\
                      .then_inc(turned_copied, 1)

                def tile_out(tile):
                    act.wait_ge(pv_done, u0 + 8 * tile + 8)
                    nc.scalar.activation(oT[:, :, tile * P:tile * P + P], AO[:, :].rearrange("p (a b) -> p a b", b=P),
                                         ACT.Copy).then_inc(att_tile, 1)

                for u in range(16):
                    act.wait_ge(max_ready, u0 + u + 1)
                    if u >= 2:
                        act.wait_ge(turned_ready, u0 + u - 1)
                    nc.scalar.activation(Pb[:, u % 2, 0:widths[u]], AS[u % 2][:, 0:widths[u]], ACT.Exp,
                                         bias=nmax[:, u % 2:u % 2 + 1], accum_out=den[:, u // 8, u % 8:u % 8 + 1])\
                      .then_inc(exp_done, 1)
                    if u == 10:
                        tile_out(0)
                    if u >= 1:
                        copy(u - 1)
                    if u in after:
                        after[u]()
                copy(15)
                tile_out(1)

            attention(0, [512] * 16, Pm, PTs, oaT, {8: lambda: mod_rows(1), 15: lambda: mod_rows(2)})

            def gate1(b):
                ev1(gates[:, 2 * b:2 * b + 2, :], view=T, func=ACT.Tanh, scale=0.5)

            attention(16, [512] * 16, Pm, PTs, obT, gates_after(gate1))
            bank[0] += 8
            act.wait_ge(bgu_zeroed, 1)
            act.dma_start(bgu[0:NE, :], A["b_gu"]).then_inc(bgu_in, 16)
            act.dma_start(bdn, A["b_dn"]).then_inc(bgu_in, 16)

            def squares_of_banks(dst, first, done, count, each=1):
                for b in range(4):
                    act.wait_ge(done, count + each * b)
                    nc.scalar.activation(dst[:, 2 * b:2 * b + 2, :],
                                         PB[(first + b) % 4][:, :].rearrange("p (a b) -> p a b", b=T), ACT.Square)\
                      .then_inc(sq_ready, 1)

            def squares_of_x(dst, updated, before, each=2):
                for b in range(4):
                    act.wait_ge(updated, before + each * (b + 1))
                    nc.scalar.activation(dst[:, 2 * b:2 * b + 2, :], xT[:, 2 * b:2 * b + 2, :], ACT.Square)\
                      .then_inc(sq_ready, 1)

            squares_of_banks(sqy, M1 + 8, bank_done, M1 + 9)
            root(3, AS[0], rstd)
            squares_of_x(sqy, x_mid, 0)
            root(4, AS[0], rstd)
            for k in range(KD):
                act.wait_ge(scaled_ready, 3 + k)
                nc.scalar.activation(hT[:, k, :], sqy[:, k, :], ACT.Identity, bias=mod[:, 24 + k, 0:1])\
                  .then_inc(h_ready, 1)
            act.wait_ge(route_pe, 1)
            nc.scalar.activation(lpart, AS[0][:, 0:T], ACT.Copy).then_inc(logits_copied, 1)
            for c in range(4):
                act.wait_ge(h2tok_t, c + 1)
                nc.scalar.activation(h2tok[:, c // 2, 512 * (c % 2):512 * (c % 2) + 512], PB[c][:, :], ACT.Copy)\
                  .then_inc(h2tok_c, 1)
            act.wait_ge(route_dve, 1)
            for tt in range(TT):
                nc.scalar.activation(prob[:, tt, :], logit[:, tt, 0:NE], ACT.Exp, bias=nm1[:, tt:tt + 1])\
                  .then_inc(route_act, 1)
            act.wait_ge(xg_t, 1)
            nc.scalar.activation(xe.rearrange("p a h c -> p (a h c)"), AO[:, :], ACT.Copy).then_inc(xe_ready, 1)
            act.wait_ge(route_dve, 7)
            act.wait_ge(small2_zeroed, 1)
            act.dma_start(wlr[:, :, 0:16], w_cols(A["w_in_2"], LR0, LR0 + 16),
                          allow_slow_non_contiguous=True).then_inc(small2_in, 16)
            act.dma_start(wlr[:, :, 16:24], w_cols(A["w_in_2"], FF0, FF0 + NH),
                          allow_slow_non_contiguous=True).then_inc(small2_in, 16)
            for j in range(4):
                act.dma_start(aw2[32 * j:32 * j + 16, :], A["alpha_w2"]).then_inc(small2_in, 16)
            n_items = act.value_load(table[0:1, ITEMS:ITEMS + 1], min_val=NE, max_val=ITEMS - 1)
            with act.Fori(0, n_items) as i:
                act.wait_ge(xg_t, i + 2)
                nc.scalar.activation(xe.rearrange("p a h c -> p (a h c)"), AO[:, :], ACT.Copy).then_inc(xe_ready, 1)
                act.wait_ge(glu_ready, i + 1)
                nc.scalar.activation(esig, glu, ACT.Tanh, scale=0.5 * 1.702).then_inc(esig_ready, 1)
                act.wait_ge(act_turned, i + 1)
                nc.scalar.activation(act_s.rearrange("p a h c -> p (a h c)"), PT[:, :], ACT.Copy)\
                  .then_inc(act_s_ready, 1)
                act.wait_ge(selwt_t, i + 1)
                nc.scalar.activation(SelWT, PT[:, 0:T], ACT.Copy).then_inc(selwt_c, 1)
                act.wait_ge(up_slot, i * RING + 2 * RING)
                nc.scalar.activation(yb, AO[:, :], ACT.Copy, scale=0.5).then_inc(yb_c, 1)
            squares_of_banks(sqf, 0, moe_done, 1, each=0)
            root(5, AS[0], rstd)
            squares_of_x(sqf, x_mid, KD)
            root(6, AS[0], rstd)

            bank[0] = 0
            ev2 = lambda dst, *a, **k: evac(bank_done2, act_evac2, dst, *a, **k)
            act.wait_ge(gla_pe, 1)
            nc.scalar.activation(glrT, PT[:, 0:T], ACT.Copy).then_inc(gla_act, 1)
            act.wait_ge(gla_pe, 2)
            for j in range(2):
                nc.scalar.activation(Z[:, j * T:j * T + T], AO[:, j * T:j * T + T], ACT.Identity,
                                     bias=col("alpha_b", j)).then_inc(gla_act, 1)
            act.wait_ge(gla_dve, 1)
            step(nc.scalar.activation(Z1, Z1, ACT.Exp, scale=-1.0))
            nc.scalar.activation(Z1, Z1, ACT.Ln, bias=C("one")).then_inc(gla_act, 1)
            for b in range(2):
                ev2(gqk[:, 2 * b:2 * b + 2, :], view=T)
            act.wait_ge(gla_dve, 2)
            nc.scalar.activation(eb, bcum, ACT.Exp).then_inc(gla_act, 1)
            nc.scalar.activation(enb, bcum, ACT.Exp, scale=-1.0).then_inc(gla_act, 1)
            nc.scalar.activation(kd, kd, ACT.Exp).then_inc(gla_act, 1)
            def token_tiles(dst):
                for tt in range(TT):
                    ev2(dst[:, tt, :])

            token_tiles(gv)
            token_tiles(gr)
            act.wait_ge(act_evac2, 6)
            nc.scalar.activation(esr, gr, ACT.Tanh, scale=0.5).then_inc(gla_act, 1)
            act.wait_ge(gla_pe, 5)
            nc.scalar.activation(kdtok, PT[:, :].rearrange("p (a b) -> p a b", b=256), ACT.Copy)\
              .then_inc(gla_act, 1)
            token_tiles(fq)
            token_tiles(fk)
            act.wait_ge(gla_pe, 8)
            og5 = og.rearrange("p t (a b v) -> p t a b v", b=2, v=P)
            for odd, src in enumerate((AO, PT)):
                nc.scalar.activation(og5[CHUNK:P, 0, :, odd, :],
                                     src[CHUNK:P, 0:256].rearrange("p (a v) -> p a v", v=P), ACT.Copy)
                ins = nc.scalar.activation(og5[:, 1, :, odd, :], src[:, 256:512].rearrange("p (a v) -> p a v", v=P),
                                           ACT.Copy)
            ins.then_inc(gla_act, 1)
            act.wait_ge(qk_sq, 2)
            nc.scalar.activation(ssq[:, 0:32], ssq[:, 0:32], ACT.Sqrt, scale=1.0 / DH, bias=C("eps"))\
              .then_inc(qk_root, 1)
            act.wait_ge(gla_dve, 6)
            nc.scalar.activation(osq, og, ACT.Square).then_inc(gla_act, 1)
            act.wait_ge(gla_dve, 7)
            nc.scalar.activation(den[:, 0, :], den[:, 0, :], ACT.Sqrt, scale=1.0 / P, bias=C("eps"))\
              .then_inc(gla_act, 1)
            token_tiles(fv)
            for tt in range(TT):
                ev2(ogT[:, :, tt * P:tt * P + P], view=P)
            for tt in range(TT):
                ev2(fqT[:, :, tt * P:tt * P + P], view=P, scale=DH ** -0.5)
                ev2(fkT[:, :, tt * P:tt * P + P], view=P)
            def gate2(b):
                B = bank[0]
                bank[0] += 1
                act.wait_ge(bank_done2, B + 1)
                for j in range(2):
                    ins = nc.scalar.activation(gate2_tile[2 * b + j], PB[B % 4][:, j * T:j * T + T], ACT.Tanh,
                                               scale=0.5, bias=half_gate_b[:, 2 * b + j:2 * b + j + 1])
                ins.then_inc(act_evac2, 1)

            attention(32, [P] * 8 + [T] * 8, Pm2, PT2, ofT, gates_after(gate2))
            bank[0] += 8
            squares_of_x(sq2, dve_evac2, KD, each=1)
            root(7, AS[0], rstd)
            for s in range(11):
                cv, ge = cv2[:, s % 2], ge2[:, s % 2]
                if s >= 2:
                    act.wait_ge(actT_ready, s - 1)
                act.wait_ge(ffn_gate, 2 * s + 1)
                nc.scalar.activation(ge, cv, ACT.Square).then_inc(ffn_act, 1)
                act.wait_ge(ffn_gate, 2 * s + 2)
                nc.scalar.activation(ge, ge, ACT.Tanh, scale=0.7978845608028654).then_inc(ffn_act, 1)
            squares_of_x(sq2, x_mid, 2 * KD)
            root(8, AS[0], rstd)

        @block.vector
        def _(dve):
            V = nc.vector
            n_step = [0]

            def step(ins):
                n_step[0] += 1
                ins.then_inc(dve_step, 1)
                dve.wait_ge(dve_step, n_step[0])

            def bc(ap, n, mid=True):
                return ap.unsqueeze(1).to_broadcast([P, n, ap.shape[-1]]) if mid else \
                    ap.unsqueeze(2).to_broadcast([P, ap.shape[-1], n])

            def scale_rows(src, dst, n, r):
                dve.wait_ge(root_ready, n)
                step(V.reciprocal(r, r))
                return V.tensor_tensor(dst, src, bc(r, KD), ALU.mult)

            cc = col("c", 0, 2 * KD).rearrange("p (k c) -> p k c", c=2)
            step(V.memset(cs, 0.0))
            dve.wait_ge(consts_in, 48)
            dve.wait_ge(cs_exp, 1)
            step(V.tensor_scalar(cse, cse, 0.5, 0.5, ALU.mult, ALU.add))
            V.tensor_tensor(cs[:, :, 0:2], cc, cse, ALU.mult).then_inc(cs_ready, 1)
            dve.wait_ge(x_in, 16)
            scale_rows(xT[:], sqx, 1, rstd).then_inc(scaled_ready, 1)
            dve.wait_ge(ctx_in, 16)
            scale_rows(ctxT, sqc, 2, rstd_c).then_inc(scaled_ready, 1)
            def modulation(g, T_bank):
                dve.wait_ge(bank_done, T_bank + 1)
                V.tensor_tensor(mod[:, 16 * g:16 * g + 16, :].rearrange("p (j f) c -> p j f c", f=4),
                                PB[T_bank % 4][:, :].rearrange("p (f j r) -> p j f r", j=4, r=32)[:, :, :, 0:2],
                                col("b_mod", 16 * g, 16).rearrange("p (j f) -> p j f", f=4).unsqueeze(3)
                                .to_broadcast([P, 4, 4, 2]), ALU.add).then_inc(dve_evac, 1)
                dve.wait_ge(dve_evac, g + 1)

            modulation(0, 1)
            V.scalar_tensor_tensor(out=A1, in0=mod[:, 8:16, :], scalar=1.0,
                                   in1=bc(col("g_pre_mix", 0, 8), 2, mid=False), op0=ALU.add, op1=ALU.mult)\
             .then_inc(mod_ready, 1)
            dve.wait_ge(mod_ready, 1)
            for k in range(KD):
                V.tensor_scalar(hcT[:, k, :], sqc[:, k, :], A1[:, k, 1:2], mod[:, k, 1:2], ALU.mult, ALU.add)\
                 .then_inc(hc_ready, 1)

            def mod_a():
                modulation(1, HEAD1 + 1)
                V.tensor_tensor(gt1, mod[:, 16:24, 0], col("g_post_mix", 0, 8), ALU.mult)

            def mod_b():
                modulation(2, G1 - 1)
                V.scalar_tensor_tensor(out=A2, in0=mod[:, 32:40, 0], scalar=1.0, in1=col("g_pre_ffn", 0, 8),
                                       op0=ALU.add, op1=ALU.mult)
                V.tensor_tensor(gt2, mod[:, 40:48, 0], col("g_post_ffn", 0, 8), ALU.mult)

            def attention(u0, widths, bias_of, Pb, after={}):
                def normalise(u):
                    dve.wait_ge(exp_done, u0 + u + 1)
                    step(V.reciprocal(dinv[:, u % 8:u % 8 + 1], den[:, u // 8, u % 8:u % 8 + 1]))
                    V.tensor_scalar(Pb[:, u % 2, 0:widths[u]], Pb[:, u % 2, 0:widths[u]], dinv[:, u % 8:u % 8 + 1],
                                    None, ALU.mult).then_inc(probs_ready, 1)

                for u in range(16):
                    w = widths[u]
                    dve.wait_ge(scores_ready, u0 + u + 1)
                    if bias_of(u) is not None:
                        b = bias_of(u)
                        step(V.tensor_tensor(AS[u % 2][:, 0:b.shape[-1]], AS[u % 2][:, 0:b.shape[-1]], b, ALU.add))
                    if u >= 2:
                        dve.wait_ge(exp_done, u0 + u - 1)
                    step(V.reduce_max(nmax[:, u % 2:u % 2 + 1], AS[u % 2][:, 0:w], AX.X))
                    V.tensor_scalar(nmax[:, u % 2:u % 2 + 1], nmax[:, u % 2:u % 2 + 1], -1.0, None, ALU.mult)\
                     .then_inc(max_ready, 1)
                    if u >= 1:
                        normalise(u - 1)
                    if u in after:
                        after[u]()
                normalise(15)

            q3 = qb.rearrange("p t (h d) -> p (t h) d", d=DH)
            k4 = kvb[:, :, 0:128]
            t1q = tmp1.rearrange("p t (h d) -> p (t h) d", d=DH)
            t2k = tmp2.rearrange("p t c -> p (t c)")[:, 0:512].rearrange("p (t c) -> p t c", c=128)
            dve.wait_ge(act_evac, evacs(BANKS1, 6, "act"))
            V.tensor_tensor(t1q, q3, q3, ALU.mult)
            step(V.tensor_tensor(t2k, k4, k4, ALU.mult))
            V.reduce_sum(ssq[:, 0:16], t1q, AX.X)
            V.reduce_sum(ssq[:, 16:24], t2k.rearrange("p t (g d) -> p t g d", d=DH), AX.X).then_inc(qk_sq, 1)
            dve.wait_ge(qk_root, 1)
            step(V.reciprocal(ssq[:, 0:24], ssq[:, 0:24]))
            V.tensor_tensor(q3, q3, bc(ssq[:, 0:16], DH, mid=False), ALU.mult)
            for i in range(4):
                ins = V.tensor_tensor(k4[:, i, :].rearrange("p (g d) -> p g d", d=DH),
                                      k4[:, i, :].rearrange("p (g d) -> p g d", d=DH),
                                      bc(ssq[:, 16 + 2 * i:18 + 2 * i], DH, mid=False), ALU.mult)
            step(ins)
            V.tensor_tensor(q3, q3, bc(row("g_q"), 16), ALU.mult)
            for i in range(4):
                ins = V.tensor_tensor(k4[:, i, :].rearrange("p (g d) -> p g d", d=DH),
                                      k4[:, i, :].rearrange("p (g d) -> p g d", d=DH), bc(row("g_k"), NKV), ALU.mult)
            step(ins)
            cos = C("cos").rearrange("p (t d) -> p t d", d=DH)
            sin = C("sin").rearrange("p (t d) -> p t d", d=DH)
            for tt in range(TT):
                for src, n, a, b in ((qb[:, tt, :], NH, tmp1[:, tt, :], tmp2[:, tt, :]),
                                     (kvb[:, tt, 0:128], NKV, rk1[:, tt, :], rk2[:, tt, :])):
                    V.tensor_tensor(a.rearrange("p (h d) -> p h d", d=DH), src.rearrange("p (h d) -> p h d", d=DH),
                                    bc(cos[:, tt, :], n), ALU.mult)
                    for half in range(2):
                        s4 = src.rearrange("p (g b f) -> p g b f", b=2, f=16)[:, :, 1 - half, :]
                        o4 = b.rearrange("p (g b f) -> p g b f", b=2, f=16)[:, :, half, :]
                        s3 = sin[:, tt, :].rearrange("p (g b f) -> p g b f", b=2, f=16)[:, :, half, :]
                        s4 = s4.rearrange("p (h g) f -> p h g f", g=2)
                        o4 = o4.rearrange("p (h g) f -> p h g f", g=2)
                        ins = V.tensor_tensor(o4, s4, s3.unsqueeze(1).to_broadcast([P, n, 2, 16]), ALU.mult)
            step(ins)
            V.tensor_tensor(qb, tmp1, tmp2, ALU.add)
            step(V.tensor_tensor(kvb[:, 0:2, 0:128], rk1, rk2, ALU.add))
            for i in range(4):
                for u in range(2):
                    ins = V.tensor_copy(kdup[:, i, :].rearrange("p (g u d) -> p g u d", u=2, d=DH)[:, :, u, :],
                                        k4[:, i, :].rearrange("p (g d) -> p g d", d=DH))
            ins.then_inc(qb_ready, 1)

            dve.wait_ge(bias_masked, 1)
            attention(0, [512] * 16, lambda u: bias[:, u // 8, u % 8, :], Pm, {10: mod_a})
            mod_b()

            attention(16, [512] * 16, lambda u: None, Pm)

            def sigmoid_gates(g):
                step(V.tensor_scalar(g, g, 0.5, 0.5, ALU.mult, ALU.add))

            def merge(B0, done, freed, freed0, ga, gb, dst, ready):
                for j in range(KD):
                    B = B0 + j
                    dve.wait_ge(done, B + 1)
                    V.tensor_tensor(ga(j), ga(j), PB[B % 4][:, 0:T], ALU.mult)
                    V.tensor_tensor(gb(j), gb(j), PB[B % 4][:, T:2 * T], ALU.mult).then_inc(freed, 1)
                    dve.wait_ge(freed, freed0 + j + 1)
                    V.tensor_tensor(dst[:, j, :], ga(j), gb(j), ALU.add).then_inc(ready, 1)

            dve.wait_ge(act_evac, evacs(BANKS1, M1, "act"))
            sigmoid_gates(gates)
            merge(M1, bank_done, dve_evac, 3, lambda j: gates[:, j, :], lambda j: gates[:, KD + j, :],
                  mergedT, merged_ready)
            dve.wait_ge(merged_ready, KD)
            V.memset(bgu, 0.0).then_inc(bgu_zeroed, 1)

            def add_to_x(src, gain):
                for k in range(KD):
                    ins = V.scalar_tensor_tensor(out=xT[:, k, :], in0=src[:, k, :], scalar=gain(k),
                                                 in1=xT[:, k, :], op0=ALU.mult, op1=ALU.add)
                    ins.then_inc(x_mid, 1)

            def scale_banks(dst, first, n, squared):
                dve.wait_ge(sq_ready, squared)
                dve.wait_ge(root_ready, n)
                step(V.reciprocal(rstd, rstd))
                for b in range(4):
                    ins = V.tensor_tensor(dst[:, 2 * b:2 * b + 2, :],
                                          PB[(first + b) % 4][:, :].rearrange("p (a b) -> p a b", b=T),
                                          bc(rstd, 2), ALU.mult)
                step(ins)

            scale_banks(yT, M1 + 8, 3, 2 + 4)
            add_to_x(yT, lambda k: gt1[:, k:k + 1])
            dve.wait_ge(x_mid, KD)
            dve.wait_ge(root_ready, 4)
            step(V.reciprocal(rstd, rstd))
            for k in range(KD):
                V.scalar_tensor_tensor(out=sqy[:, k, :], in0=xT[:, k, :], scalar=A2[:, k:k + 1], in1=rstd,
                                       op0=ALU.mult, op1=ALU.mult).then_inc(scaled_ready, 1)

            V.memset(OHb, 0.0)
            V.memset(logit, SENTINEL)
            V.memset(POSI, -FAR)
            step(V.memset(WI, 0.0))
            dve.wait_ge(logits_turned, 1)
            step(V.reduce_sum(logit[:, :, 0:NE], AS[1][:, 0:T].rearrange("p (t j e) -> p t e j", j=4, e=NE), AX.X))
            step(V.tensor_tensor(logit[:, :, 0:NE], logit[:, :, 0:NE], bc(row("b_router"), TT), ALU.add))
            for tt in range(TT):
                ins = V.max(top8[:, tt, :], logit[:, tt, 0:NE])
            step(ins)
            V.tensor_scalar(nm1, top8[:, :, 0], -1.0, None, ALU.mult).then_inc(route_dve, 1)
            step(V.memset(top8[:, :, TOPK:8], SENTINEL))
            for tt in range(TT):
                ins = V.match_replace(mark[:, tt, :], top8[:, tt, :], logit[:, tt, :], 3.0e38)
            step(ins)
            step(V.tensor_tensor(sel, mark[:, :, 0:NE], logit[:, :, 0:NE], ALU.is_gt))
            dve.wait_ge(route_act, 2)
            step(V.tensor_tensor(prob, prob, sel, ALU.mult))
            step(V.reduce_sum(lsum, prob, AX.X))
            step(V.reciprocal(linv, lsum))
            V.tensor_tensor(WI[:, :, 0:NE], prob, bc(linv, NE, mid=False), ALU.mult).then_inc(route_dve, 1)
            dve.wait_ge(route_dve, 2)
            dve.wait_ge(route_pe, 2)
            step(V.tensor_scalar(mark[:, :, 0:NE], sel, FAR, -FAR - 1.0, ALU.mult, ALU.add))
            V.tensor_tensor(POSI[:, :, 0:NE], mark[:, :, 0:NE],
                            AS[1][:, 0:TT * NE].rearrange("p (t e) -> p t e", e=NE), ALU.add)\
             .then_inc(route_dve, 1)
            n_e = eblk[:, 0:1]
            nov = eblk[:, 1:2]
            step(V.tensor_copy(n_e, AO[0:NE, 0:1]))
            step(V.tensor_scalar(nov, n_e, float(CAP), None, ALU.is_gt))
            for m in range(2, T // CAP):
                step(V.scalar_tensor_tensor(out=nov, in0=n_e, scalar=float(m * CAP), in1=nov, op0=ALU.is_gt,
                                            op1=ALU.add))
            V.tensor_copy(eblk[:, 2:3], nov).then_inc(route_dve, 1)
            dve.wait_ge(route_pe, 3)
            ov_end, ov_start = eblk[:, 3:4], eblk[:, 4:5]
            step(V.tensor_copy(ov_end, AO[0:NE, 1:2]))
            step(V.tensor_tensor(ov_start, ov_end, nov, ALU.subtract))
            io = C("iota")[0:NE, 0:EXTRA]
            g1, g2, jj = eblk[:, 16:32], eblk[:, 32:48], eblk[:, 48:64]
            V.memset(OH[:, ITEMS:ITEMS + 1], 0.0)
            V.tensor_copy(OH[:, 0:NE], ident[0:NE, 0:NE])
            step(V.tensor_scalar(g1, io, ov_start, None, ALU.is_ge))
            step(V.scalar_tensor_tensor(out=OH[:, NE:ITEMS], in0=io, scalar=ov_end, in1=g1, op0=ALU.is_lt,
                                        op1=ALU.mult))
            step(V.tensor_scalar(g2, io, ov_start, 1.0, ALU.subtract, ALU.add))
            step(V.tensor_tensor(jj, g2, OH[:, NE:ITEMS], ALU.mult))
            V.tensor_scalar(jj, jj, -float(CAP), None, ALU.mult).then_inc(route_dve, 1)
            dve.wait_ge(route_pe, 4)
            V.tensor_copy(posT, PT[0:NE, 0:T])
            V.tensor_copy(wT, PT[0:NE, T:2 * T]).then_inc(route_dve, 1)
            dve.wait_ge(route_pe, 6)
            V.tensor_copy(POSI[:, :, NE:ITEMS], AO[:, 8:8 + TT * EXTRA].rearrange("p (t e) -> p t e", e=EXTRA))
            V.tensor_copy(WI[:, :, NE:ITEMS], AO[:, 64:64 + TT * EXTRA].rearrange("p (t e) -> p t e", e=EXTRA))
            V.tensor_copy(table[0:1, 0:NE], C("iota")[0:1, 0:NE])
            V.tensor_copy(table[0:1, NE:ITEMS], AO[0:1, 128:128 + EXTRA])
            V.tensor_scalar(table[0:1, ITEMS:ITEMS + 1], AO[0:1, 160:161], float(NE), None, ALU.add)
            V.memset(SelWT, 0.0).then_inc(selwt_c, 1)
            V.memset(SelW, 0.0).then_inc(route_dve, 1)
            V.memset(yb, 0.0).then_inc(yb_c, 1)
            dve.wait_ge(route_dve, 7)

            def one_hots(at):
                for tt in range(TT):
                    ins = V.tensor_scalar(Sel[:, tt, :], C("iota")[:, 0:CAP], POSI[:, tt, at], None, ALU.is_equal)
                ins.then_inc(sel_ready, 1)

            def weighted_one_hots(at):
                for tt in range(TT):
                    ins = V.tensor_scalar(SelW[:, tt, :], C("iota"), POSI[:, tt, at], WI[:, tt, at],
                                          ALU.is_equal, ALU.mult)
                ins.then_inc(selw_ready, 1)

            def expert_one_hot(at):
                V.tensor_copy(OHb[0:NE, :], OH[:, at].to_broadcast([NE, CAP])).then_inc(ohb_ready, 1)

            one_hots(slice(0, 1))
            expert_one_hot(slice(0, 1))
            weighted_one_hots(slice(0, 1))
            dve.wait_ge(gathered, 1)
            V.tensor_copy(xg, PT[:, :]).then_inc(xg_ready, 1)
            n_items = dve.value_load(table[0:1, ITEMS:ITEMS + 1], min_val=NE, max_val=ITEMS - 1)
            with dve.Fori(0, n_items) as i:
                STEPS = 2
                k_step = [0]

                def mstep(ins):
                    k_step[0] += 1
                    ins.then_inc(moe_dve, 1)
                    dve.wait_ge(moe_dve, i * STEPS + k_step[0])

                dve.wait_ge(gathered, i + 1)
                one_hots(bass.ds(i + 1, 1))
                dve.wait_ge(bias_added, i + 1)
                expert_one_hot(bass.ds(i + 1, 1))
                dve.wait_ge(xg_t, i + 1)
                dve.wait_ge(gathered, i + 2)
                V.tensor_copy(xg, PT[:, :]).then_inc(xg_ready, 1)
                dve.wait_ge(up_slot, i * RING + (RING + 4))
                V.tensor_scalar(glu, AS[0][:, :], 7.0, None, ALU.min).then_inc(glu_ready, 1)
                mstep(V.tensor_scalar(lin, AS[1][:, :], 7.0, -7.0, ALU.min, ALU.max))
                dve.wait_ge(glu_ready, i + 1)
                mstep(V.scalar_tensor_tensor(out=lin, in0=lin, scalar=1.0, in1=glu, op0=ALU.add, op1=ALU.mult))
                dve.wait_ge(esig_ready, i + 1)
                V.scalar_tensor_tensor(out=act_t, in0=esig, scalar=1.0, in1=lin, op0=ALU.add, op1=ALU.mult)\
                 .then_inc(actv_ready, 1)
                dve.wait_ge(selwt_t, i + 1)
                weighted_one_hots(bass.ds(i + 1, 1))

            scale_banks(fT, 0, 5, 2 + 4 * 3)
            add_to_x(fT, lambda k: gt2[:, k:k + 1])
            dve.wait_ge(x_mid, 2 * KD)

            def norm_x(n, gain):
                dve.wait_ge(root_ready, n)
                step(V.reciprocal(rstd, rstd))
                for k in range(KD):
                    V.scalar_tensor_tensor(out=hT[:, k, :], in0=xT[:, k, :], scalar=col(gain, k), in1=rstd,
                                           op0=ALU.mult, op1=ALU.mult).then_inc(h_ready, 1)

            norm_x(6, "norm_mix")
            V.tensor_scalar(half_gate_b, col("gate_b", 0, 2 * KD), 0.5, None, ALU.mult)
            dve.wait_ge(gla_act, 3)
            dve.wait_ge(gla_pe, 3)
            zf = Z[:, 512:528].rearrange("p (t h) -> p t h", h=NH)
            step(V.reduce_sum(zf, AS[1][:, 0:T].rearrange("p (t j e) -> p t e j", j=4, e=32)[:, :, 16:24, :], AX.X))
            step(V.tensor_tensor(zf, zf, bc(row("forget_b"), TT), ALU.add))
            V.scalar_tensor_tensor(out=Z1, in0=Z, scalar=-1.0, in1=Z, op0=ALU.mult, op1=ALU.max).then_inc(gla_dve, 1)
            dve.wait_ge(gla_act, 4)
            step(V.scalar_tensor_tensor(out=Z, in0=Z, scalar=0.0, in1=Z1, op0=ALU.min, op1=ALU.subtract))
            step(V.tensor_scalar(Z[:, 0:512], Z[:, 0:512], 1.0 / TAU, None, ALU.mult))
            for j in range(2):
                ins = V.tensor_tensor_scan(bcum[:, j, :], C("carry"), Z[:, j * T:j * T + T], 0.0, ALU.mult, ALU.add)
            step(ins)
            b4 = bcum.rearrange("p j (n l) -> p (j n) l", l=CHUNK)
            V.tensor_tensor(kd.rearrange("p j (n l) -> p (j n) l", l=CHUNK),
                            b4[:, :, CHUNK - 1:CHUNK].to_broadcast([P, 2 * NCH, CHUNK]), b4, ALU.subtract)\
             .then_inc(gla_dve, 1)
            dve.wait_ge(gla_act, 7)
            dve.wait_ge(act_evac2, 2)
            V.scalar_tensor_tensor(out=qe, in0=gqk[:, 0:2, :], scalar=DH ** -0.5, in1=eb, op0=ALU.mult, op1=ALU.mult)
            V.tensor_tensor(ke, gqk[:, 2:4, :], enb, ALU.mult)
            V.tensor_tensor(kd, gqk[:, 2:4, :], kd, ALU.mult).then_inc(gla_dve, 1)
            dve.wait_ge(gla_act, 8)
            step(V.tensor_scalar(esr, esr, 0.5, 0.5, ALU.mult, ALU.add))
            step(V.tensor_tensor(esr, esr, gr, ALU.mult))
            step(V.tensor_tensor(esr, esr, bc(row("gla_out"), TT), ALU.mult))
            dve.wait_ge(gla_pe, 4)
            for odd in range(2):
                ins = V.tensor_tensor(AT.rearrange("p t (a b l) -> p (t a) b l", b=2, l=CHUNK)[:, :, odd, :],
                                      AS[odd][:, 0:256].rearrange("p (a l) -> p a l", l=CHUNK),
                                      C("gla_mask").unsqueeze(1).to_broadcast([P, TT * 2, CHUNK]), ALU.mult)
            ins.then_inc(gla_dve, 1)
            dve.wait_ge(gla_pe, 7)
            kv = lambda n: kv_bank[n][:, kv_at[n]:kv_at[n] + 256].rearrange("p (j v) -> p j v", v=P)
            step(V.tensor_copy(St[:, 0], kv(0)))
            for n in range(1, 3):
                for j in range(2):
                    ins = V.scalar_tensor_tensor(out=St[:, n, j, :], in0=St[:, n - 1, j, :],
                                                 scalar=eb[:, j, CHUNK * n + CHUNK - 1:CHUNK * n + CHUNK],
                                                 in1=kv(n)[:, j, :], op0=ALU.mult, op1=ALU.add)
                if n < 2:
                    step(ins)
                else:
                    ins.then_inc(gla_dve, 1)
            dve.wait_ge(act_evac2, 10)
            dve.wait_ge(gla_pe, 5)
            for src, at in ((fq, 0), (fk, 16)):
                s3 = src.rearrange("p t (h d) -> p (t h) d", d=DH)
                f3 = fsq.rearrange("p t (h d) -> p (t h) d", d=DH)
                step(V.tensor_tensor(f3, s3, s3, ALU.mult))
                ins = V.reduce_sum(ssq[:, at:at + 16], f3, AX.X)
                if at == 0:
                    step(ins)
            ins.then_inc(qk_sq, 1)
            dve.wait_ge(gla_act, 10)
            V.tensor_copy(og[0:CHUNK, 0, :], AS[0][0:CHUNK, :])
            V.tensor_tensor(og[CHUNK:P, 0, :], og[CHUNK:P, 0, :], AS[0][CHUNK:P, :], ALU.add)
            V.tensor_tensor(og[:, 1, :], og[:, 1, :], AS[1][:, :], ALU.add).then_inc(gla_dve, 1)
            dve.wait_ge(gla_act, 11)
            V.reduce_sum(den[:, 0, :], osq.rearrange("p t (h v) -> p (t h) v", v=P), AX.X).then_inc(gla_dve, 1)
            dve.wait_ge(qk_root, 2)
            step(V.reciprocal(ssq[:, 0:32], ssq[:, 0:32]))
            for src, at in ((fq, 0), (fk, 16)):
                s3 = src.rearrange("p t (h d) -> p (t h) d", d=DH)
                ins = V.tensor_tensor(s3, s3, bc(ssq[:, at:at + 16], DH, mid=False), ALU.mult)
            step(ins)
            for src, gain in ((fq, "fox_q"), (fk, "fox_k")):
                s3 = src.rearrange("p t (h d) -> p (t h) d", d=DH)
                ins = V.tensor_tensor(s3, s3, bc(row(gain), 16), ALU.mult)
            ins.then_inc(qb_ready, 1)
            dve.wait_ge(gla_act, 12)
            step(V.reciprocal(dinv, den[:, 0, :]))
            o3 = og.rearrange("p t (h v) -> p (t h) v", v=P)
            step(V.tensor_tensor(o3, o3, bc(dinv, P, mid=False), ALU.mult))
            V.tensor_tensor(og, og, esr, ALU.mult).then_inc(gla_dve, 1)
            dve.wait_ge(gla_pe, 9)
            step(V.tensor_copy(cq, PT[:, 0:TT * NH].rearrange("p (t h) -> p t h", h=NH)))
            for pair in range(4):
                dve.wait_ge(gla_pe, 10 + pair)
                bankp = c_banks[pair]
                for hh in range(2):
                    h = 2 * pair + hh
                    for tt in range(TT):
                        n = P * (tt + 1)
                        ins = V.tensor_scalar(Cb[tt][:, h, :], bankp[:, hh * T:hh * T + n], -1.0, cq[:, tt, h:h + 1],
                                              ALU.mult, ALU.add)
                ins.then_inc(cb_ready, 1)
            dve.wait_ge(cb_ready, 4)
            for tt in range(TT):
                ins = V.tensor_tensor(Cb[tt][:, :, P * tt:P * tt + P], Cb[tt][:, :, P * tt:P * tt + P],
                                      bc(C("causal"), NH), ALU.add)
            step(ins)
            attention(32, [P] * 8 + [T] * 8, lambda u: Cb[u // 8][:, u % 8, :], Pm2)

            dve.wait_ge(act_evac2, evacs(BANKS2, M2, "act"))
            for lo, n in gate_spans:
                sigmoid_gates(region(lo, 256 * n))
            merge(M2, bank_done2, dve_evac2, 0, lambda j: gate2_tile[j], lambda j: gate2_tile[KD + j], merged2,
                  merged_ready2)
            for b in range(4):
                dve.wait_ge(bank_done2, M2 + 8 + b + 1)
                V.tensor_tensor(xT[:, 2 * b:2 * b + 2, :], xT[:, 2 * b:2 * b + 2, :],
                                PB[(M2 + 8 + b) % 4][:, :].rearrange("p (a b) -> p a b", b=T), ALU.add)\
                 .then_inc(dve_evac2, 1)
            dve.wait_ge(dve_evac2, KD + 4)
            norm_x(7, "norm_ffn")

            for s in range(11):
                B = M2 + 12 + 2 * s
                gf, cv, ge = gf2[:, s % 2], cv2[:, s % 2], ge2[:, s % 2]
                if s >= 2:
                    dve.wait_ge(actT_ready, s - 1)
                for j in range(2):
                    dve.wait_ge(bank_done2, B + j + 1)
                    ft = 2 * s + j
                    a_ = PB[(B + j) % 4][:, 0:T]
                    V.tensor_scalar(gf[:, j, :], PB[(B + j) % 4][:, T:2 * T], 0.5, None, ALU.mult)
                    w = lambda i: col("conv_w", i * F2T + ft)
                    step(V.tensor_scalar(cv[:, j, :], a_, w(2), col("conv_b", ft), ALU.mult, ALU.add))
                    step(V.scalar_tensor_tensor(out=cv[:, j, 1:T], in0=a_[:, 0:T - 1], scalar=w(1), in1=cv[:, j, 1:T],
                                                op0=ALU.mult, op1=ALU.add))
                    V.scalar_tensor_tensor(out=cv[:, j, 2:T], in0=a_[:, 0:T - 2], scalar=w(0),
                                           in1=cv[:, j, 2:T], op0=ALU.mult, op1=ALU.add).then_inc(dve_evac2, 1)
                dve.wait_ge(dve_evac2, KD + 4 + 2 * s + 2)
                V.tensor_tensor(gf, gf, cv, ALU.mult).then_inc(ffn_gate, 1)
                dve.wait_ge(ffn_act, 2 * s + 1)
                step(V.tensor_scalar(ge, ge, 0.044715, 1.0, ALU.mult, ALU.add))
                V.tensor_tensor(ge, ge, cv, ALU.mult).then_inc(ffn_gate, 1)
                dve.wait_ge(ffn_act, 2 * s + 2)
                V.scalar_tensor_tensor(out=actT[:, 2 * s:2 * s + 2, :], in0=ge, scalar=1.0, in1=gf,
                                       op0=ALU.add, op1=ALU.mult).then_inc(actT_ready, 1)
            for b in range(4):
                dve.wait_ge(down_slots, 5 + b + 1)
                V.tensor_tensor(xT[:, 2 * b:2 * b + 2, :], xT[:, 2 * b:2 * b + 2, :],
                                PB[b][:, :].rearrange("p (a b) -> p a b", b=T), ALU.add).then_inc(x_mid, 2)
            dve.wait_ge(x_mid, 3 * KD)
            dve.wait_ge(root_ready, 8)
            step(V.reciprocal(rstd, rstd))
            for k in range(KD):
                V.scalar_tensor_tensor(out=fT[:, k, :], in0=xT[:, k, :], scalar=col("norm_final", k), in1=rstd,
                                       op0=ALU.mult, op1=ALU.mult).then_inc(final_ready, 1)

        @block.tensor
        def _(pe):
            mm = nc.tensor.matmul

            def sum_squares(sq, bank, n):
                for k in range(KD):
                    if n <= 2 and k == 0:
                        pe.wait_ge(sq_ready, n)
                    elif n > 2 and k % 2 == 0:
                        pe.wait_ge(sq_ready, 2 + 4 * (n - 3) + k // 2 + 1)
                    ins = mm(bank[:, 0:T], ones, sq[:, k, :], start=k == 0, stop=k == KD - 1)
                ins.then_inc(sum_ready, 1)

            pe.wait_ge(consts_in, 48)
            sum_squares(sqx, AS[0], 1)
            sum_squares(sqc, AS[1], 2)
            B = [0]
            state = [BANKS1, bank_done, act_evac, dve_evac, landed]

            def bank():
                banks, _, act_s_, dve_s_, _ = state
                n = B[0]
                B[0] += 1
                if n >= 4:
                    who = banks[n - 4]
                    pe.wait_ge(act_s_ if who == "act" else dve_s_, evacs(banks, n - 3, who))
                return PB[n % 4]

            def need(n):
                if state[0] is BANKS1:
                    pe.wait_ge(landed[n % RING], 16 * (n // RING + 1))
                else:
                    pe.wait_ge(landed2[n % RING], land2(n))

            def features(W, src, c0, K=KD):
                pb = bank()
                for c in range(2):
                    for k in range(K):
                        ins = mm(pb[:, c * T:c * T + T], W[:, k, (c0 + c) * P:(c0 + c) * P + P], src[:, k, :],
                                 start=k == 0, stop=k == K - 1)
                ins.then_inc(state[1], 1)

            def tokens(W, src, tt, n=512):
                pb = bank()
                for k in range(KD):
                    ins = mm(pb[:, 0:n], src[:, k, tt * P:tt * P + P], W[:, k, 0:n], start=k == 0, stop=k == KD - 1)
                ins.then_inc(state[1], 1)

            def mod_part(pb, n0, ks):
                for k in ks:
                    if k % 2 == 0:
                        need(n0 + k // 2)
                    W = slot(n0 + k // 2, 2, 2048)
                    for j in range(4):
                        ins = mm(pb[32 * j:32 * j + 32, :], cs[:, k, :], W[:, k % 2, 512 * j:512 * j + 512],
                                 start=k == 0, stop=k == KD - 1)
                    if k % 2:
                        ins.then_inc(mod_slots, 1)

            def mod_turn(n_rows):
                pe.wait_ge(act_evac, n_rows)
                pb = bank()
                for f in range(4):
                    ins = nc.tensor.transpose(pb[:, f * P:f * P + P], modrow[:, f * P:f * P + P], ident)
                ins.then_inc(bank_done, 2)

            pe.wait_ge(cs_ready, 1)
            mod_part(bank(), 0, range(KD))
            mod_turn(1)

            pe.wait_ge(h_ready, KD)
            need(4)
            for src in (hT, hcT):
                if src is hcT:
                    pe.wait_ge(hc_ready, KD)
                pb = bank()
                for tt in range(TT):
                    for k in range(KD):
                        ins = mm(pb[:, tt * 256:tt * 256 + 256], src[:, k, tt * P:tt * P + P],
                                 slot(4, KD, 256)[:, k, :], start=k == 0, stop=k == KD - 1)
                ins.then_inc(bank_done, 1)
            need(5)
            for tt in range(TT):
                tokens(slot(5, KD, 512), hT, tt)
            need(6)
            for src in (hT, hcT):
                for b in range(2):
                    features(slot(6, KD, 512), src, 2 * b)
            pe.wait_ge(qb_ready, 1)
            for tt in range(TT):
                pb = bank()
                for c in range(4):
                    ins = nc.tensor.transpose(pb[:, c * P:c * P + P], qb[:, tt, c * P:c * P + P], ident)
                ins.then_inc(bank_done, 1)
            for g in range(NKV):
                pb = bank()
                for i in range(4):
                    ins = nc.tensor.transpose(pb[:, i * P:i * P + P], kdup[:, i, g * P:g * P + P], ident)
                ins.then_inc(bank_done, 1)
            need(7)
            for src in (hT, hcT):
                for tt in range(TT):
                    tokens(slot(7, KD, 512), src, tt)
            need(8)
            for b in range(2):
                features(slot(8, KD, 512), hT, 2 * b)

            def attention(u0, widths, scores, value, Pb, PTb, after):
                def s(u):
                    if u >= 2:
                        pe.wait_ge(exp_done, u0 + u - 1)
                    for q, k, at in scores(u):
                        ins = mm(AS[u % 2][:, at:at + k.shape[-1]], q, k, start=True, stop=True)
                    ins.then_inc(scores_ready, 1)

                def turn(u):
                    pe.wait_ge(probs_ready, u0 + u + 1)
                    if u >= 1:
                        pe.wait_ge(turned_copied, u0 + u)
                    for c in range(widths[u] // P):
                        ins = nc.tensor.transpose(PT[:, c * P:c * P + P], Pb[:, u % 2, c * P:c * P + P], ident)
                    ins.then_inc(turned_ready, 1)

                def pv(u):
                    h = u % NH
                    pe.wait_ge(turned_copied, u0 + u + 1)
                    if h == 0 and u0 + u:
                        pe.wait_ge(att_tile, (u0 + u) // 8)
                    n = widths[u] // P
                    for c in range(n):
                        ins = mm(AO[DH * (h % 2):DH * (h % 2) + DH, (h // 2) * P:(h // 2) * P + P], value(u, c),
                                 PTb[:, u % 2, c * P:c * P + P], start=c == 0, stop=c == n - 1)
                    ins.then_inc(pv_done, 1)

                s(0)
                for u in range(16):
                    if u < 15:
                        s(u + 1)
                    if u >= 1:
                        turn(u - 1)
                    if u >= 2:
                        pv(u - 2)
                    if u in after:
                        after[u]()
                turn(15)
                pv(14)
                pv(15)
                if 16 in after:
                    after[16]()

            def part(ap3, h):
                return ap3[DH * (h % 2):DH * (h % 2) + DH, h // 2]

            def na_scores(u):
                h, tt = u % NH, u // NH
                return [(qaT[:, h, tt * P:tt * P + P], kaT[h // 4][:, h // 2 % 2, :], 0)]

            mod_bank = [None]

            def mod_some(n0, ks):
                if ks[0] == 0:
                    mod_bank[0] = bank()
                mod_part(mod_bank[0], n0, ks)

            na_after = {u: (lambda u=u: mod_some(9, [u])) for u in range(8)}
            na_after[9] = lambda: mod_turn(evacs(BANKS1, HEAD1 + 1, "act"))
            na_after.update({u: (lambda u=u: mod_some(13, [2 * (u - 11), 2 * (u - 11) + 1])) for u in range(11, 15)})
            na_after[16] = lambda: mod_turn(evacs(BANKS1, G1 - 1, "act"))
            pe.wait_ge(act_evac, evacs(BANKS1, HEAD1, "act"))
            attention(0, [512] * 16, na_scores, lambda u, c: Va[:, c, (u % 8) * DH:(u % 8) * DH + DH],
                      Pm, PTs, na_after)
            def gqa_scores(u):
                h, tt = u % NH, u // NH
                q = qbT[DH * (h % 2):DH * (h % 2) + DH, tt, h // 2, :]
                return [(q, kbT[DH * (h % 2):DH * (h % 2) + DH, h // 4, :], 0)]

            def gate1(b):
                n = 17 + b // 2
                if b % 2 == 0:
                    need(n)
                features(slot(n, KD, 512), hT, 2 * (b % 2))

            pe.wait_ge(act_evac, evacs(BANKS1, G1, "act"))
            attention(16, [512] * 16, gqa_scores, lambda u, c: kvb[:, c, 128 + DH * (u % 8 // 4):192 + DH * (u % 8 // 4)],
                      Pm, PTs, gates_after(gate1))

            def branches(na, nb, oa, ob, ready_sem, ready_n):
                pe.wait_ge(ready_sem, ready_n)
                need(na)
                need(nb)
                for j in range(KD):
                    pb = bank()
                    for c, (n, o) in enumerate(((na, oa), (nb, ob))):
                        for k in range(4):
                            ins = mm(pb[:, c * T:c * T + T], slot(n, 4, D)[:, k, j * P:j * P + P], o[:, k, :],
                                     start=k == 0, stop=k == 3)
                    ins.then_inc(state[1], 1)

            branches(21, 22, oaT, obT, att_tile, 4)
            pe.wait_ge(merged_ready, KD)
            for n in range(2):
                need(23 + n)
                for b in range(2):
                    features(slot(23 + n, KD, 512), mergedT, 2 * b)
            sum_squares(sqy, AS[0], 3)
            sum_squares(sqy, AS[0], 4)

            pe.wait_ge(router_in, 16)
            pe.wait_ge(h_ready, 2 * KD)
            for kk in range(2):
                for j in range(4):
                    ins = mm(AS[0][32 * j:32 * j + 32, 0:T], wr[:, 2 * j + kk, :], hT[:, 2 * j + kk, :],
                             start=kk == 0, stop=kk == 1)
            ins.then_inc(route_pe, 1)
            for c in range(4):
                for kk in range(4):
                    k = 4 * (c % 2) + kk
                    ins = nc.tensor.transpose(PB[c][:, kk * P:kk * P + P], hT[:, k, (c // 2) * P:(c // 2) * P + P],
                                              ident)
                ins.then_inc(h2tok_t, 1)
                if c == 0:
                    pe.wait_ge(logits_copied, 1)
                    for tt in range(TT):
                        ins = nc.tensor.transpose(AS[1][:, tt * P:tt * P + P], lpart[:, tt * P:tt * P + P], ident)
                    ins.then_inc(logits_turned, 1)
            pe.wait_ge(route_dve, 2)
            for tt in range(TT):
                for s in range(tt + 1):
                    mm(AS[1][:, tt * NE:tt * NE + NE], tri[:, s, tt * P:tt * P + P], sel[:, s, :],
                       start=s == 0, stop=s == tt)
            for s in range(TT):
                ins = mm(AO[0:NE, 0:1], sel[:, s, :], ones[:, 0:1], start=s == 0, stop=s == 1)
            ins.then_inc(route_pe, 1)
            pe.wait_ge(route_dve, 4)
            mm(AO[0:NE, 1:2], C("tri32")[0:NE, :], eblk[:, 2:3], start=True, stop=True).then_inc(route_pe, 1)
            for tt in range(TT):
                nc.tensor.transpose(PT[0:NE, tt * P:tt * P + P], POSI[:, tt, 0:NE], ident)
                ins = nc.tensor.transpose(PT[0:NE, T + tt * P:T + tt * P + P], WI[:, tt, 0:NE], ident)
            ins.then_inc(route_pe, 1)
            pe.wait_ge(route_dve, 6)
            for tt in range(TT):
                mm(AO[:, 8 + tt * EXTRA:8 + (tt + 1) * EXTRA], posT[:, tt * P:tt * P + P], OH[:, NE:ITEMS],
                   start=True, stop=False)
                mm(AO[:, 8 + tt * EXTRA:8 + (tt + 1) * EXTRA], ones[0:NE, :], eblk[:, 48:64], start=False, stop=True)
            for tt in range(TT):
                ins = mm(AO[:, 64 + tt * EXTRA:64 + (tt + 1) * EXTRA], wT[:, tt * P:tt * P + P], OH[:, NE:ITEMS],
                         start=True, stop=True)
            ins.then_inc(route_pe, 1)
            mm(AO[0:1, 128:128 + EXTRA], C("eid")[0:NE, :], OH[:, NE:ITEMS], start=True, stop=True)
            mm(AO[0:1, 160:161], eblk[:, 2:3], ones[0:NE, 0:1], start=True, stop=True).then_inc(route_pe, 1)
            pe.wait_ge(h2tok_c, 4)
            pe.wait_ge(bgu_in, 32)
            for k in range(KD):
                ins = mm(sum_at(k), bdn[:, k * P:k * P + P], wT[:, :], start=k % 2 == 0, stop=False,
                         skip_group_check=True)
            ins.then_inc(up_slot, RING)

            halves = [(slice(CAP * b, CAP * b + CAP), slice(512 * b, 512 * b + 512)) for b in range(2)]

            def gather():
                for tt in range(TT):
                    for parts, feats in halves:
                        ins = mm(PT[parts, :], Sel[:, tt, :], h2tok[:, tt, feats], start=tt == 0, stop=tt == TT - 1)
                ins.then_inc(gathered, 1)

            def turn(bank_, src):
                for c in range(4):
                    ins = nc.tensor.transpose(bank_[:, c * P:c * P + P], src[:, c * P:c * P + P], ident)
                return ins

            def combine():
                for k in (0, 4, 1, 5, 2, 6, 3, 7):
                    half = slice(CAP * (k // 4), CAP * (k // 4) + CAP)
                    ins = mm(sum_at(k), yb[half, (k % 4) * P:(k % 4) * P + P], SelWT[half, :],
                             start=False, stop=False, skip_group_check=True)
                return ins

            pe.wait_ge(sel_ready, 1)
            gather()

            pe.wait_ge(xg_ready, 1)
            turn(AO, xg).then_inc(xg_t, 1)
            pe.wait_ge(route_dve, 7)
            n_items = pe.value_load(table[0:1, ITEMS:ITEMS + 1], min_val=NE, max_val=ITEMS - 1)
            with pe.Fori(0, n_items) as i:
                pe.wait_ge(ohb_ready, i + 1)
                for n in range(2):
                    for parts, feats in halves:
                        ins = mm(AS[n][parts, :], OHb[:, :], bgu[:, n * D + feats.start:n * D + feats.stop],
                                 start=True, stop=False)
                ins.then_inc(bias_added, 1)
                pe.wait_ge(xe_ready, i + 1)
                for s in range(4):
                    pe.wait_ge(landed[s], i * 16 + 16 * prior[s] + 16)
                    W = slot(s, 2, 2 * D)
                    for kk in range(2):
                        k = 2 * s + kk
                        for n in range(2):
                            for parts, feats in halves:
                                ins = mm(AS[n][parts, :], xe[:, k % 4, k // 4, :],
                                         W[:, kk, n * D + feats.start:n * D + feats.stop],
                                         start=False, stop=k == KD - 1)
                    ins.then_inc(up_slot, 1)
                    if s == 2:
                        pe.wait_ge(sel_ready, i + 2)
                        pe.wait_ge(selwt_c, i + 1)
                        gather()
                pe.wait_ge(xg_ready, i + 2)
                pe.wait_ge(yb_c, i + 1)
                turn(AO, xg).then_inc(xg_t, 1)
                combine()
                pe.wait_ge(actv_ready, i + 1)
                turn(PT, act_t).then_inc(act_turned, 1)
                pe.wait_ge(act_s_ready, i + 1)
                pe.wait_ge(xe_ready, i + 2)
                for s in range(4, 6):
                    pe.wait_ge(landed[s], i * 16 + 16 * prior[s] + 16)
                    W = slot(s, 4, D)
                    for kk in range(4):
                        for parts, feats in halves:
                            ins = mm(AO[parts, :], act_s[:, kk, s - 4, :], W[:, kk, feats],
                                     start=s == 4 and kk == 0, stop=s == 5 and kk == 3)
                    ins.then_inc(up_slot, 1)
                    if s == 4:
                        pe.wait_ge(selw_ready, i + 1)
                        for tt in range(TT):
                            ins = nc.tensor.transpose(PT[:, tt * P:tt * P + P], SelW[:, tt, :], ident)
                        ins.then_inc(selwt_t, 1)
            pe.wait_ge(selwt_c, n_items + 1)
            pe.wait_ge(yb_c, n_items + 1)
            combine().then_inc(moe_done, 1)
            sum_squares(sqf, AS[0], 5)
            sum_squares(sqf, AS[0], 6)

            B[0] = 0
            state[:] = [BANKS2, bank_done2, act_evac2, dve_evac2, landed2]
            pe.wait_ge(h_ready, 3 * KD)
            pe.wait_ge(small2_in, 96)
            for kk in range(2):
                for j in range(4):
                    ins = mm(PT[32 * j:32 * j + 32, 0:T], wlr[:, 2 * j + kk, :], hT[:, 2 * j + kk, :],
                             start=kk == 0, stop=kk == 1)
            ins.then_inc(gla_pe, 1)
            pe.wait_ge(gla_act, 1)
            for j in range(2):
                ins = mm(AO[:, j * T:j * T + T], aw2[:, j * P:j * P + P], glrT, start=True, stop=True)
            ins.then_inc(gla_pe, 1)
            for tt in range(TT):
                ins = nc.tensor.transpose(AS[1][:, tt * P:tt * P + P], glrT[:, tt * P:tt * P + P], ident)
            ins.then_inc(gla_pe, 1)
            need(0)
            for b in range(2):
                features(slot(0, KD, 512), hT, 2 * b)

            def token_slot(n):
                need(n)
                for tt in range(TT):
                    tokens(slot(n, KD, 512), hT, tt)

            token_slot(1)
            token_slot(2)
            pe.wait_ge(gla_dve, 3)
            for h in range(4):
                for n in range(NCH):
                    q = part(qe, h)[:, n * CHUNK:(n + 1) * CHUNK]
                    k_ = part(ke, h)[:, n * CHUNK:(n + 1) * CHUNK]
                    m0 = CHUNK * (n % 2)
                    at = ((n // 2) * 2 + h // 2) * CHUNK
                    ins = mm(AS[h % 2][m0:m0 + CHUNK, at:at + CHUNK], k_, q, start=True, stop=True)
            ins.then_inc(gla_pe, 1)
            for tt in range(TT):
                for j in range(2):
                    ins = nc.tensor.transpose(PT[:, tt * 256 + j * P:tt * 256 + (j + 1) * P],
                                              kd[:, j, tt * P:tt * P + P], ident)
            ins.then_inc(gla_pe, 1)
            token_slot(3)
            pe.wait_ge(gla_act, 9)
            pe.wait_ge(act_evac2, 4)
            for n in range(3):
                m0 = CHUNK * (n % 2)
                for h in range(4):
                    d0 = DH * (h % 2)
                    at = kv_at[n] + (h // 2) * P
                    ins = mm(kv_bank[n][d0:d0 + DH, at:at + P], kdtok[m0:m0 + CHUNK, n // 2, h * DH:h * DH + DH],
                             gv[m0:m0 + CHUNK, n // 2, h * P:h * P + P], start=True, stop=True)
                if n:
                    ins.then_inc(gla_pe, 1)
            token_slot(4)
            pe.wait_ge(gla_dve, 5)
            for n in range(NCH):
                m0 = CHUNK * (n % 2)
                for h in range(4):
                    ins = mm(AS[n // 2][m0:m0 + CHUNK, h * P:h * P + P],
                             AT[m0:m0 + CHUNK, n // 2, h * CHUNK:(h + 1) * CHUNK],
                             gv[m0:m0 + CHUNK, n // 2, h * P:h * P + P], start=True, stop=True)
                    if n:
                        at = (n // 2) * 256 + (h // 2) * P
                        ins = mm([AO, PT][h % 2][m0:m0 + CHUNK, at:at + P], part(qe, h)[:, n * CHUNK:(n + 1) * CHUNK],
                                 St[DH * (h % 2):DH * (h % 2) + DH, n - 1, h // 2, :], start=True, stop=True)
            ins.then_inc(gla_pe, 1)
            token_slot(5)
            pe.wait_ge(gla_act, 10)
            logf = Z[:, 512:528].rearrange("p (t h) -> p t h", h=NH)
            for tt in range(TT):
                for s in range(tt + 1):
                    ins = mm(PT[:, tt * NH:(tt + 1) * NH], tri[:, s, tt * P:tt * P + P], logf[:, s, :],
                             start=s == 0, stop=s == tt)
            ins.then_inc(gla_pe, 1)
            for pair in range(4):
                if pair == 1:
                    pe.wait_ge(gla_dve, 6)
                if pair == 2:
                    pe.wait_ge(cb_ready, 1)
                for hh in range(2):
                    for s in range(TT):
                        lf = logf[:, s, 2 * pair + hh:2 * pair + hh + 1].to_broadcast([P, P])
                        ins = mm(c_banks[pair][:, hh * T:hh * T + T], lf, tri[:, s, :], start=s == 0, stop=s == 1)
                ins.then_inc(gla_pe, 1)
            pe.wait_ge(gla_dve, 8)
            for tt in range(TT):
                pb = bank()
                for c in range(4):
                    ins = nc.tensor.transpose(pb[:, c * P:c * P + P], og[:, tt, c * P:c * P + P], ident)
                ins.then_inc(bank_done2, 1)
            pe.wait_ge(qb_ready, 2)
            for tt in range(TT):
                for src in (fq, fk):
                    pb = bank()
                    for c in range(4):
                        ins = nc.tensor.transpose(pb[:, c * P:c * P + P], src[:, tt, c * P:c * P + P], ident)
                    ins.then_inc(bank_done2, 1)

            def fox_scores(u):
                h, tt = u % NH, u // NH
                return [(part(fqT, h)[:, tt * P:tt * P + P], part(fkT, h)[:, 0:P * (tt + 1)], 0)]

            def gate2(b):
                n = 6 + b // 2
                if b % 2 == 0:
                    need(n)
                features(slot(n, KD, 512), hT, 2 * (b % 2))

            pe.wait_ge(act_evac2, G2)
            pe.wait_ge(cb_ready, 4)
            attention(32, [P] * 8 + [T] * 8, fox_scores, lambda u, c: fv[:, c, (u % 8) * DH:(u % 8) * DH + DH],
                      Pm2, PT2, gates_after(gate2))
            branches(10, 11, ogT, ofT, att_tile, 6)
            pe.wait_ge(merged_ready2, KD)
            for n in range(2):
                need(12 + n)
                for b in range(2):
                    features(slot(12 + n, KD, 512), merged2, 2 * b)
            sum_squares(sq2, AS[0], 7)
            pe.wait_ge(h_ready, 4 * KD)
            for n in range(11):
                need(UP0 + n)
                W = slot(UP0 + n, KD, 512)
                for j in range(2):
                    pb = bank()
                    for c in range(2):
                        for k in range(KD):
                            ins = mm(pb[:, c * T:c * T + T], W[:, k, c * 256 + j * P:c * 256 + j * P + P],
                                     hT[:, k, :], start=k == 0, stop=k == KD - 1)
                    ins.then_inc(bank_done2, 1)
            pe.wait_ge(dve_evac2, KD + 4 + 22)
            for n in range(6):
                need(DN0 + n)
                pe.wait_ge(actT_ready, min(2 * n + 2, 11))
                K = stream2[DN0 + n].shape[1]
                W = slot(DN0 + n, K, D)
                for j in range(KD):
                    for k in range(K):
                        ins = mm(PB[j // 2][:, (j % 2) * T:(j % 2) * T + T], W[:, k, j * P:j * P + P],
                                 actT[:, 4 * n + k, :], start=n == 0 and k == 0 and j % 2 == 0, stop=n == 5 and k == K - 1,
                                 skip_group_check=True)
                    if n == 5 and j % 2:
                        ins.then_inc(down_slots, 1)
                if n < 5:
                    ins.then_inc(down_slots, 1)
            sum_squares(sq2, AS[0], 8)


INPUTS = ["w_mod", "w_in", "w_out_a", "w_out_b", "w_o", "w_router", "b_gu", "b_dn", "w_gu", "w_dn"]
RENAMED = {"w_in_2": "w_in_2", "alpha_w2": "gla_alpha_w2_2", "w_gla": "w_gla_branch_2", "w_fox": "w_fox_branch_2",
           "w_out_2": "w_out_2", "w_up": "w_up_2", "w_down": "w_down_2"}


def kernel(**inputs):
    from concourse.bass_utils import run_bass_kernel_spmd as run
    import concourse.bacc as bacc

    get = lambda name: np.asarray(inputs[name])

    def features_first(a):
        return np.ascontiguousarray(a.T.reshape(KD, P, -1).transpose(1, 0, 2))

    def columns(a):
        return a.reshape(-1, P).T

    arrays = {name: np.ascontiguousarray(get(name)[0]) for name in INPUTS}
    arrays |= {name: np.ascontiguousarray(get(theirs)[0]) for name, theirs in RENAMED.items()}
    arrays["xT"] = features_first(get("x")[0])
    arrays["ctxT"] = features_first(get("ctx")[0])
    arrays["cst"] = constants()
    both = np.stack([get("c")[0], get("c_ctx")])
    parts = [columns(get(n)[0]) for n in ("b_mod", "g_pre_mix", "g_post_mix", "g_pre_ffn", "g_post_ffn",
                                          "norm_mix_g_2", "gla_alpha_b_2", "gate_b_2", "norm_ffn_g_2", "conv_w_2",
                                          "conv_b_2")]
    parts += [columns(get("norm_final_g_2")), features_first(both).reshape(P, 2 * KD)]
    arrays["cols"] = np.ascontiguousarray(np.concatenate(parts, axis=1))
    arrays["rows"] = np.concatenate([get(n)[0].reshape(-1) for n in (
        "g_qnorm", "g_knorm", "fox_q_norm_g_2", "fox_k_norm_g_2", "gla_out_norm_g_2", "fox_forget_b_2", "b_router")])
    padded = np.pad(get("rpb")[0].reshape(NH * 15, 31), ((0, 0), (48, 48)))
    arrays["rpb"] = np.ascontiguousarray(np.broadcast_to(padded[:, None, :], (NH * 15, GRID_W, 127)))

    nc = bacc.Bacc("TRN2", target_bir_lowering=False, num_devices=1)
    A = {n: nc.dram_tensor(n + "_dram", a.shape, mybir.dt.from_np(a.dtype), kind="ExternalInput").ap()
         for n, a in arrays.items()}
    out = nc.dram_tensor("out_dram", (P, KD, T), F32, kind="ExternalOutput").ap()
    two_blocks(nc, A, out)
    r = run(nc, [{n + "_dram": a for n, a in arrays.items()}], core_ids=[0])
    got = r.results[0]["out_dram"]
    return np.ascontiguousarray(got.transpose(2, 1, 0)).reshape(1, T, D)
```
